# Optimizing a Trainium2 kernel written in Bass

```python
import jax, jax.numpy as jnp
from jax import lax
import numpy as np

D_MODEL = 1024
BATCH = 1
SEQ = 4096
DEPTH = 1
DEC_BATCH = 1
DEC_SEQ = 32
PAST_LEN = 4096

CHUNK = 64
D_MIX = D_MODEL
D_A = D_MIX // 2
D_B = D_MIX - D_A
CONV_A = 3
CONV_B = 31
RMS_EPS = 1e-6
LN_EPS = 1e-5
D_IN = 4 * D_A + 3 * D_B
SPLITS = [D_A, 2 * D_A, 3 * D_A, 4 * D_A, 4 * D_A + D_B, 4 * D_A + 2 * D_B]

kernel_name = "hybrid_shortconv_conformerconv_stream_step"

def rms_norm(x, g):
    x32 = x.astype(jnp.float32)
    y = x32 * lax.rsqrt(jnp.mean(x32 * x32, axis=-1, keepdims=True) + RMS_EPS)
    return (y * g.astype(jnp.float32)).astype(x.dtype)

def layer_norm(x, g, b):
    x32 = x.astype(jnp.float32)
    mu = jnp.mean(x32, axis=-1, keepdims=True)
    xc = x32 - mu
    var = jnp.mean(xc * xc, axis=-1, keepdims=True)
    y = xc * lax.rsqrt(var + LN_EPS) * g.astype(jnp.float32) + b.astype(jnp.float32)
    return y.astype(x.dtype)

def causal_dwconv(hist, u, w):
    k1 = w.shape[0] - 1
    xp = jnp.concatenate([hist.astype(u.dtype), u], axis=1)
    y = lax.conv_general_dilated(
        xp, w[:, None, :].astype(u.dtype), window_strides=(1,), padding='VALID',
        dimension_numbers=('NWC', 'WIO', 'NWC'), feature_group_count=u.shape[-1])
    return y, xp[:, xp.shape[1] - k1:, :]

def mixer_layer(x, hist_a, hist_b, norm_g, w_in, conv_a_w, conv_b_w, conv_b_bias,
                ln_b_g, ln_b_b, w_out):
    hn = rms_norm(x, norm_g)
    proj = jnp.einsum('btd,de->bte', hn, w_in.astype(hn.dtype))
    h_a, b_a, c_a, z_a, a_b, g_b, z_b = jnp.split(proj, SPLITS, axis=-1)
    conv_a, new_a = causal_dwconv(hist_a, c_a * h_a, conv_a_w)
    out_a = b_a * conv_a * jax.nn.silu(z_a)
    v_b = a_b * jax.nn.sigmoid(g_b)
    conv_b, new_b = causal_dwconv(hist_b, v_b, conv_b_w)
    s_b = jax.nn.silu(layer_norm(conv_b + conv_b_bias.astype(conv_b.dtype), ln_b_g, ln_b_b))
    out_b = s_b * jax.nn.silu(z_b)
    mixed = jnp.concatenate([out_a, out_b], axis=-1)
    y = jnp.einsum('bte,ed->btd', mixed, w_out.astype(mixed.dtype))
    return x + y, new_a, new_b

def setup_inputs(seed: int = 0) -> dict:
    key = jax.random.key(seed)
    ks = jax.random.split(key, 14)
    f32 = jnp.float32
    return {
        "x_prompt": jax.random.normal(ks[0], (BATCH, SEQ, D_MODEL), f32),
        "x_sample": jax.random.normal(ks[1], (DEC_BATCH, DEC_SEQ, D_MODEL), f32),
        "state_conv_a": jax.random.normal(ks[2], (DEPTH, DEC_BATCH, CONV_A - 1, D_A), f32),
        "state_conv_b": 0.5 * jax.random.normal(ks[3], (DEPTH, DEC_BATCH, CONV_B - 1, D_B), f32),
        "norm_g": 1.0 + 0.02 * jax.random.normal(ks[4], (DEPTH, D_MODEL), f32),
        "w_in": jax.random.normal(ks[5], (DEPTH, D_MODEL, D_IN), f32) * D_MODEL ** -0.5,
        "conv_a_w": jax.random.normal(ks[6], (DEPTH, CONV_A, D_A), f32) * CONV_A ** -0.5,
        "conv_b_w": jax.random.normal(ks[7], (DEPTH, CONV_B, D_B), f32) * CONV_B ** -0.5,
        "conv_b_bias": 0.02 * jax.random.normal(ks[8], (DEPTH, D_B), f32),
        "ln_b_g": 1.0 + 0.02 * jax.random.normal(ks[9], (DEPTH, D_B), f32),
        "ln_b_b": 0.02 * jax.random.normal(ks[10], (DEPTH, D_B), f32),
        "w_out": jax.random.normal(ks[11], (DEPTH, D_MIX, D_MODEL), f32) * D_MIX ** -0.5,
        "final_norm_g": 1.0 + 0.02 * jax.random.normal(ks[12], (D_MODEL,), f32),
    }

def reference(x_prompt, x_sample, state_conv_a, state_conv_b, norm_g, w_in, conv_a_w,
              conv_b_w, conv_b_bias, ln_b_g, ln_b_b, w_out, final_norm_g):
    hp, hs = x_prompt, x_sample
    bp = x_prompt.shape[0]
    pa_list, pb_list, sa_list, sb_list = [], [], [], []
    for l in range(DEPTH):
        zero_a = jnp.zeros((bp, CONV_A - 1, D_A), hp.dtype)
        zero_b = jnp.zeros((bp, CONV_B - 1, D_B), hp.dtype)
        hp, pa, pb = mixer_layer(hp, zero_a, zero_b, norm_g[l], w_in[l], conv_a_w[l],
                                 conv_b_w[l], conv_b_bias[l], ln_b_g[l], ln_b_b[l], w_out[l])
        hs, sa, sb = mixer_layer(hs, state_conv_a[l], state_conv_b[l], norm_g[l], w_in[l],
                                 conv_a_w[l], conv_b_w[l], conv_b_bias[l], ln_b_g[l],
                                 ln_b_b[l], w_out[l])
        pa_list.append(pa); pb_list.append(pb); sa_list.append(sa); sb_list.append(sb)
    y_prompt = rms_norm(hp, final_norm_g)
    y_sample = rms_norm(hs, final_norm_g)
    new_conv_a_prompt = jnp.stack(pa_list, axis=0)
    new_conv_b_prompt = jnp.stack(pb_list, axis=0)
    new_conv_a_sample = jnp.stack(sa_list, axis=0)
    new_conv_b_sample = jnp.stack(sb_list, axis=0)
    return (y_prompt, y_sample, new_conv_a_prompt, new_conv_b_prompt, new_conv_a_sample, new_conv_b_sample)


_drawn_inputs = setup_inputs


def setup_inputs(seed=0):
    import zlib

    import numpy as np

    out = dict(_drawn_inputs(seed))
    spreads = {}
    factors = {'conv_b_bias': 6.37, 'ln_b_g': 8.0, 'ln_b_b': 8.0, 'final_norm_g': 2.888}
    for name, (base, spread) in spreads.items():
        noise = np.random.default_rng([zlib.crc32(name.encode()), seed]).standard_normal(out[name].shape)
        drawn = base * np.exp(spread * noise) if base else spread * noise
        out[name] = __import__('jax').numpy.asarray(drawn.astype(out[name].dtype))
    for name, factor in factors.items():
        out[name] = (out[name] * factor).astype(out[name].dtype)
    return out
```

```python
import concourse.bass as bass
from concourse import mybir
from contextlib import ExitStack

F32 = mybir.dt.float32
F32R = mybir.dt.float32r
I32 = mybir.dt.int32
ALU = mybir.AluOpType
ACT = mybir.ActivationFunctionType

P = 128
D = 1024
KC = D // P
DA = 512
JT = DA // P
SEQ, SAMPLE = 4096, 32
KA, KB = 3, 31
HA, HB = KA - 1, KB - 1
RMS_EPS, LN_EPS = 1e-6, 1e-5
RMS_SCALE = D ** -0.5

PASSES = 2
BLOCKS = 9
TB = 460
PAD = BLOCKS * TB - SEQ - SAMPLE
S0, P0 = PAD, PAD + SAMPLE
TOK = BLOCKS * TB
ROWS = [P, P, P, TB - 3 * P]

VW = HB + SAMPLE + HB + (TB - P0)
VH = VW - TB - HB
UW = HA + TB
UH0 = UW - (HA + SAMPLE + HA + TB - P0)
ACCW = VW - HB
AC0 = ACCW - TB

TILES = [("g", 0), ("a", 0), ("g", 1), ("a", 1), ("zb", 0), ("zb", 1), ("h", 0), ("c", 0),
         ("b", 0), ("z", 0), ("h", 1), ("c", 1), ("b", 1), ("z", 1)]
SECTION = {"h": 0, "b": 1, "c": 2, "z": 3, "a": 4, "g": 5, "zb": 6}
M = len(TILES)
AT = {t: m for m, t in enumerate(TILES)}
ACT_TILES = [m for m, (k, _) in enumerate(TILES) if k in ("g", "zb", "h", "z")]
PROJ_BANKS = 4
SLOT = 2 * D
LEAD = 3
TAPS = [(0, k) for k in range(13)]
_a, _b = [(1, k) for k in range(KB)], [(0, k) for k in range(13, KB)]
for _k in range(KB):
    TAPS.append(_a[_k])
    if _k < len(_b):
        TAPS.append(_b[_k])
NT = len(TAPS)
TAP_AT = {t: x for x, t in enumerate(TAPS)}
TAP_STOPS = {1: 13, 3: 28, 5: 39, 8: 45, 9: 57, 12: NT}
TRANSPOSE_AT = {3: 0, 5: 1, 9: 2, 11: 3}

OB = 512
RT = OB // P
OBLOCKS = SEQ // OB
LN_OPS = 20
RSQRT_SEED = 1597463007.0


def build_program(nc, A):
    ctx = ExitStack()
    with ctx:
        def sb(name, shape, dt=F32, scope=ctx):
            return scope.enter_context(nc.sbuf_tensor(name, shape, dt))

        def sem(name):
            return ctx.enter_context(nc.semaphore(name))

        conv_d = nc.dram_tensor("conv_spill", [DA, TOK], F32).ap()
        zb_d = nc.dram_tensor("zb_spill", [DA, TOK], F32).ap()
        outa_d = nc.dram_tensor("outa_spill", [DA, TOK], F32).ap()

        W = sb("w_split", [P, 12 * SLOT], F32R)
        raw = sb("w_raw", [P, 2, D])
        ident = sb("ident", [P, P])
        mean_w = sb("mean_w", [P, P])
        gain = sb("gain", [P, KC])
        wb = sb("conv_b_taps", [P, JT, KB])
        bias_b = sb("conv_b_bias_sb", [P, JT])
        wa = sb("conv_a_taps", [P, JT, KA])
        hist_b = sb("hist_b", [P, JT, HB])
        hist_a = sb("hist_a", [P, JT, HA])
        ln_g = sb("ln_g", [P, JT])
        ln_b = sb("ln_b", [P, JT])
        minus_half = sb("minus_half", [P, 1])
        eps = sb("rms_eps", [P, 1])
        ssq = sb("row_mean_sq", [P, 4])
        mean_sq = sb("row_mean_sq_eps", [P, 4])
        rstd = sb("rstd", [P, 4])
        early = ExitStack()
        W2 = sb("w_split_2", [P, 2 * SLOT], F32R, early)
        xT = [sb(f"xT{q}", [P, 2, KC, TB], F32R, early) for q in range(2)]
        xrow = sb("x_rows", [P, 2, D], F32, early)
        v = sb("v", [P, 2, VW], F32, early)
        u = sb("u", [P, 2, UW], F32, early)
        tmp = sb("gates", [P, 2, TB], F32, early)
        acc = sb("conv_b_acc", [P, 2, ACCW], F32, early)
        szb = sb("szb", [P, TB], F32, early)
        ca = sb("conv_a_acc", [P, TB], F32, early)
        early.close()
        mix2 = sb("mixed_1", [P, 2, 2 * JT, OB], F32R)
        cb = sb("cb", [P, 2, JT, OB])
        zt = sb("zt", [P, 2, JT, OB])
        oa = sb("oa", [P, 2, JT, OB])
        hrow = sb("h_rows", [P, 2, D])
        fgain = sb("final_gain", [P, D])
        ta = sb("ln_tmp_a", [P, 2, OB])
        tb = sb("ln_tmp_b", [P, 2, OB])

        def slot(m):
            t, n = (W, m) if m < 12 else (W2, m - 12)
            return t[:, n * SLOT:n * SLOT + D], t[:, n * SLOT + D:(n + 1) * SLOT]

        mix1 = W[:, 8 * SLOT:12 * SLOT].rearrange("p (l e t) -> p l e t", l=2, t=OB)
        MIX = [mix1, mix2[:, :, :, :]]

        ps = ctx.enter_context(nc.psum_tensor("ps", [P, 8, 512], F32))

        def turned(r):
            return ps[:, 4 + 2 * (r % 2):6 + 2 * (r % 2), :].rearrange("p b (c t) -> p (b c) t", t=P)

        def out_pair(s):
            return ps[:, 2 * s:2 * s + 2, :].rearrange("p b t -> p (b t)")

        const_in = sem("const_in")
        ready0 = sem("pool_consts_ready")
        x_in = [sem(f"x_rows_in_{s}") for s in range(2)]
        x_sumsq = sem("x_sumsq")
        x_ms = sem("x_mean_square")
        x_rstd = sem("x_rstd")
        x_scaled = sem("x_scaled")
        x_turned = sem("x_turned")
        x_hi = sem("x_hi")
        x_lo = sem("x_lo")
        w_in_s = [sem(f"w_raw_in_{s}") for s in range(2)]
        w_scaled = sem("w_scaled")
        w_hi = sem("w_hi")
        w_lo = sem("w_lo")
        projected = sem("projected")
        act_evac = sem("act_evacuated")
        edges = sem("window_edges")
        v_ready = sem("v_ready")
        taps_done = sem("taps_done")
        gated = sem("gated_steps")
        conv_out = sem("conv_out")
        conv_out0 = sem("conv_out_sample")
        zb_out = sem("zb_out")
        outa_out = sem("outa_out")
        state_out = sem("state_out")
        fg_in = sem("final_gain_in")
        ld = [sem(f"ln_loads_{s}") for s in range(2)]
        ln = sem("ln_steps")
        ln_mean = sem("ln_mean")
        ln_sq = sem("ln_squares")
        ln_var = sem("ln_var")
        ln_silu = sem("ln_silu")
        a_hi = sem("mixed_a_hi")
        b_hi = sem("mixed_b_hi")
        out_done = sem("rows_multiplied")
        res_in = [sem(f"residual_in_{s}") for s in range(2)]
        h_done = sem("h_done")
        h_sumsq = sem("h_sumsq")
        h_ms = sem("h_mean_square")
        h_rstd = sem("h_rstd")
        y_done = sem("y_done")
        y_out = [sem(f"y_out_{s}") for s in range(2)]

        def need(eng, s, value):
            if not (isinstance(value, int) and value <= 0):
                eng.wait_ge(s, value)

        def v_count(p, i, j):
            return 20 * p + 2 * (j + 1) if first(i) else 20 * p + 3 + 2 * i + j

        STEP = {"u": (2, 1), "taps": (5, 4), "b": (7, 5), "out": (9, 6)}

        def gated_count(p, i, j, what, back=0):
            if first(i):
                return 114 * p + 9 * j + STEP[what][0] - back
            return 114 * p + 6 + 12 * i + 6 * j + STEP[what][1] - back

        def gated_count_before(p, i, what):
            if first(i):
                return gated_count(p - 1, BLOCKS - 1, 1, what) if p else 0
            return 114 * p + 12 * i + STEP[what][1]

        def edge_count(p, i):
            return 21 * p + 5 if first(i) else 21 * p + 5 + 2 * i

        def first(i):
            return isinstance(i, int) and i == 0

        def run_blocks(eng, block):
            for p in range(PASSES):
                block(p, 0, BLOCKS * p, p)
                pairs = (BLOCKS - 1) // 2 - p
                with eng.Fori(0, pairs) as it:
                    for o in range(2):
                        i = 2 * it + (1 + o)
                        block(p, i, i + BLOCKS * p, (BLOCKS * p + 1 + o) % 2)
                for i in range(1 + 2 * pairs, BLOCKS):
                    block(p, i, i + BLOCKS * p, (BLOCKS * p + i) % 2)

        LAST = PASSES * BLOCKS - 1

        def last(n):
            return isinstance(n, int) and n == LAST

        def ln_cols(L):
            return S0 if isinstance(L, int) and L == 0 else P0 - OB + L * OB

        def ln_width(L):
            return P if isinstance(L, int) and L == 0 else OB

        def run_steps(eng, step):
            for L in (0, 1, 2):
                step(L, L % 2)
            with eng.Fori(0, (OBLOCKS - 4) // 2) as it:
                for o in range(2):
                    step(2 * it + (3 + o), (3 + o) % 2)
            for L in (OBLOCKS - 1, OBLOCKS):
                step(L, L % 2)

        def row_tiles(L):
            if isinstance(L, int) and L == 0:
                return [(0, 0, SAMPLE)]
            return [(4 * L - 3 + r, (1 + r) % 2, P) for r in range(RT)]

        def is_last(L):
            return isinstance(L, int) and L == OBLOCKS

        def ln_event(L, k):
            return LN_OPS * L + k

        def before_rows(L):
            if isinstance(L, int):
                return 0 if L <= 0 else 4 * L - 3
            return 4 * L - 3

        block = ctx.enter_context(nc.Block())

        @block.sync
        def _(sp):
            chan = lambda t: t.rearrange("(j p) k -> p j k", p=P)
            consts = [(wb[:, :, :], chan(A["conv_b_w"])), (wa[:, :, :], chan(A["conv_a_w"])),
                      (hist_b[:, :, :], chan(A["state_conv_b"])), (hist_a[:, :, :], chan(A["state_conv_a"])),
                      (bias_b[:, :], A["conv_b_bias"]), (gain[:, :], A["norm_g"]),
                      (ln_g[:, :], A["ln_b_g"]), (ln_b[:, :], A["ln_b_b"])]

            def load_x(N, i, r):
                s = r % 2
                need(sp, x_turned, 4 * N + r - 1)
                if r == 0:
                    cuts = [0, S0, P0, P]
                    for a, b in zip(cuts, cuts[1:]):
                        if first(i) and a < P0:
                            src = A["x_sample"][0:b - a, :]
                        else:
                            src = A["x_prompt"][bass.ds(TB * i - P0 + a, b - a), :]
                        sp.dma_start(xrow[a:b, s, :], src).then_inc(x_in[s], 16)
                else:
                    src = A["x_prompt"][bass.ds(TB * i - P0 + P * r, ROWS[r]), :]
                    sp.dma_start(xrow[0:ROWS[r], s, :], src).then_inc(x_in[s], 16)

            def load_w(p, m):
                c = M * p + m
                need(sp, w_lo, c - 1)
                if p < PASSES:
                    k, j = TILES[m]
                    src = A["w_in"][SECTION[k] * JT + 2 * p + j]
                else:
                    src = A["w_out"][P * m:P * (m + 1), :]
                sp.dma_start(raw[:, c % 2, :], src).then_inc(w_in_s[c % 2], 16)

            def spill(dram, p, j, nj=1):
                return dram[P * (2 * p + j):P * (2 * p + j + nj), :].rearrange("(j p) t -> p j t", p=P)

            def store_conv(p, i, n):
                sp.wait_ge(taps_done, NT * n + NT)
                dst = spill(conv_d, p, 0, 2)
                if first(i):
                    sp.dma_start(dst[:, :, S0:P0], acc[:, :, 0:SAMPLE]).then_inc(conv_out0, 16)
                    sp.dma_start(dst[:, :, P0:TB], acc[:, :, AC0 + P0:]).then_inc(conv_out, 16)
                else:
                    sp.dma_start(dst[:, :, bass.ds(TB * i, TB)], acc[:, :, AC0:]).then_inc(conv_out, 16)

            def store_zb(p, i, n, j):
                sp.wait_ge(act_evac, 8 * n + 3 + j)
                sp.dma_start(spill(zb_d, p, j)[:, 0, bass.ds(TB * i, TB)], szb[:, :]).then_inc(zb_out, 16)

            def store_outa(p, i, n, j):
                sp.wait_ge(gated, gated_count(p, i, j, "out"))
                sp.dma_start(spill(outa_d, p, j)[:, 0, bass.ds(TB * i, TB)], tmp[:, 1, :]).then_inc(outa_out, 16)

            def store_states(p, i, kind):
                vs, us = (HB + SAMPLE - HB, UH0 + SAMPLE) if kind == "sample" else (VW - HB, UW - HA)
                sp.wait_ge(v_ready, v_count(p, i, 1))
                sp.dma_start(spill(A[f"new_b_{kind}"], p, 0, 2), v[:, :, vs:vs + HB]).then_inc(state_out, 16)
                sp.wait_ge(gated, gated_count(p, i, 1, "u"))
                sp.dma_start(spill(A[f"new_a_{kind}"], p, 0, 2), u[:, :, us:us + HA]).then_inc(state_out, 16)

            def proj_block(p, i, n, q):
                nxt = i + 1 if not isinstance(i, int) else (i + 1) % BLOCKS
                if not last(n):
                    load_x(n + 1, nxt, 0)
                    load_x(n + 1, nxt, 1)
                if first(i):
                    for m in range(2 + 2 * (p == 0), 6):
                        load_w(p, m)
                if not first(i):
                    if not (isinstance(i, int) and i == 1):
                        store_conv(p, i - 1, n - 1)
                    else:
                        store_conv(p, 0, n - 1)
                if first(i):
                    load_w(p, 6)
                    load_w(p, 7)
                if not last(n):
                    load_x(n + 1, nxt, 2)
                if last(n):
                    load_w(2, 0)
                    load_w(2, 1)
                store_zb(p, i, n, 0)
                if first(i):
                    load_w(p, 8)
                if last(n):
                    load_w(2, 2)
                store_zb(p, i, n, 1)
                if first(i):
                    load_w(p, 9)
                if last(n):
                    for m in (3, 4, 5, 6):
                        load_w(2, m)
                if not last(n):
                    load_x(n + 1, nxt, 3)
                if first(i):
                    for m in (10, 11, 12):
                        load_w(p, m)
                store_outa(p, i, n, 0)
                if first(i):
                    load_w(p, 13)
                if last(n):
                    load_w(2, 7)
                store_outa(p, i, n, 1)
                if first(i):
                    store_states(p, i, "sample")
                if isinstance(i, int) and i == BLOCKS - 1:
                    store_states(p, i, "prompt")
                    store_conv(p, i, n)
                    if not last(n):
                        load_w(p + 1, 0)
                        load_w(p + 1, 1)

            def blocks():
                for p in range(PASSES):
                    proj_block(p, 0, BLOCKS * p, None)
                    proj_block(p, 1, BLOCKS * p + 1, None)
                    with sp.Fori(2, BLOCKS - 1) as i:
                        proj_block(p, i, i + BLOCKS * p, None)
                    proj_block(p, BLOCKS - 1, BLOCKS * p + BLOCKS - 1, None)

            load_x(0, 0, 0)
            load_x(0, 0, 1)
            load_w(0, 0)
            load_w(0, 1)
            for dst, src in consts:
                sp.dma_start(dst, src).then_inc(const_in, 16)
            load_x(0, 0, 2)
            load_w(0, 2)
            load_x(0, 0, 3)
            load_w(0, 3)
            blocks()

            sp.wait_ge(projected, M * (LAST + 1))
            sp.wait_ge(taps_done, NT * (LAST + 1))
            sp.wait_ge(gated, gated_count(1, BLOCKS - 1, 1, "out"))
            sp.wait_ge(conv_out, 16 * (LAST + 1))
            sp.wait_ge(conv_out0, 16 * PASSES)
            sp.wait_ge(zb_out, 32 * (LAST + 1))
            sp.wait_ge(outa_out, 32 * (LAST + 1))
            sp.wait_ge(state_out, 64 * PASSES)

            def load_ln(L, s):
                need(sp, ln, ln_event(L - 2, LN_OPS) if not isinstance(L, int) or L >= 2 else 0)
                w, c = ln_width(L), ln_cols(L)
                for t, dram in ((cb, conv_d), (oa, outa_d), (zt, zb_d)):
                    src = dram.rearrange("(j p) t -> p j t", p=P)[:, :, bass.ds(c, w)]
                    sp.dma_start(t[:, s, :, 0:w], src).then_inc(ld[s], 16)

            def load_residual(R, s, rows):
                need(sp, h_done, R - 1)
                src = A["x_sample"] if isinstance(R, int) and R == 0 else \
                    A["x_prompt"][bass.ds(P * (R - 1), P), :]
                sp.dma_start(raw[0:rows, s, :], src).then_inc(res_in[s], 16)

            def store_y(R, s, rows):
                sp.wait_ge(y_done, R + 1)
                dst = A["y_sample"] if isinstance(R, int) and R == 0 else \
                    A["y_prompt"][bass.ds(P * (R - 1), P), :]
                sp.dma_start(dst, hrow[0:rows, s, :]).then_inc(y_out[s], 16)

            def step(L, s):
                if not (isinstance(L, int) and L + 2 > OBLOCKS):
                    load_ln(L + 2, s)
                for R, rs, rows in row_tiles(L):
                    if not (is_last(L) and isinstance(R, int) and R == 4 * OBLOCKS):
                        load_residual(R + 1, (rs + 1) % 2, P)
                    store_y(R, rs, rows)

            load_ln(0, 0)
            load_ln(1, 1)
            sp.dma_start(fgain[:, :], A["final_norm_g"].to_broadcast([P, D])).then_inc(fg_in, 16)
            sp.wait_ge(w_lo, M * PASSES + KC)
            load_residual(0, 0, SAMPLE)
            run_steps(sp, step)
            sp.wait_ge(y_out[0], 16 * (2 * OBLOCKS + 1))
            sp.wait_ge(y_out[1], 16 * 2 * OBLOCKS)

        @block.gpsimd
        def _(pool):
            pool.memset(ident[:, :], 0.0).then_inc(ready0, 1)
            pool.memset(mean_w[:, :], 1.0 / DA).then_inc(ready0, 1)
            pool.memset(minus_half[:, :], -0.5).then_inc(ready0, 1)
            pool.memset(eps[:, :], RMS_EPS).then_inc(ready0, 1)
            pool.wait_ge(ready0, 4)
            pool.affine_select(out=ident[:, :], in_=ident[:, :], compare_op=ALU.not_equal, fill=1.0,
                               base=0, pattern=[[-1, P]], channel_multiplier=1).then_inc(ready0, 1)

            def row_rstd(r, rows, sumsq, ms, done, count):
                pool.wait_ge(sumsq, count)
                pool.tensor_tensor(mean_sq[0:rows, r:r + 1], ssq[0:rows, r:r + 1], eps[0:rows, :],
                                   ALU.add).then_inc(ms, 1)
                pool.wait_ge(ms, count)
                pool.tensor_tensor(rstd[0:rows, r:r + 1], mean_sq[0:rows, r:r + 1],
                                   minus_half[0:rows, :], ALU.pow).then_inc(done, 1)

            def scale_w(p, m):
                c = M * p + m
                pool.wait_ge(w_in_s[c % 2], 16 * (c // 2 + 1))
                w = raw[:, c % 2, :].rearrange("p (k c) -> p k c", k=KC)
                pool.tensor_tensor(w, w, gain[:, :].unsqueeze(2).to_broadcast([P, KC, P]),
                                   ALU.mult).then_inc(w_scaled, 1)

            def proj_block(p, i, n, q):
                for r in range(4):
                    if first(i):
                        for m in ((2, 3), (4, 5), (6, 7, 8), (9, 10))[r]:
                            scale_w(p, m)
                    if not last(n):
                        row_rstd(r, ROWS[r], x_sumsq, x_ms, x_rstd, 4 * n + 5 + r)
                if first(i):
                    for m in (11, 12, 13):
                        scale_w(p, m)
                if isinstance(i, int) and i == BLOCKS - 1 and not last(n):
                    scale_w(p + 1, 0)
                    scale_w(p + 1, 1)

            row_rstd(0, P, x_sumsq, x_ms, x_rstd, 1)
            pool.wait_ge(const_in, 128)
            scale_w(0, 0)
            for r in (1, 2, 3):
                row_rstd(r, ROWS[r], x_sumsq, x_ms, x_rstd, 1 + r)
                if r == 1:
                    scale_w(0, 1)
            for p in range(PASSES):
                proj_block(p, 0, BLOCKS * p, None)
                with pool.Fori(1, BLOCKS - 1) as i:
                    proj_block(p, i, i + BLOCKS * p, None)
                proj_block(p, BLOCKS - 1, BLOCKS * p + BLOCKS - 1, None)

            def step(L, s):
                for R, rs, rows in row_tiles(L):
                    row_rstd(rs, rows, h_sumsq, h_ms, h_rstd, R + 1)

            run_steps(pool, step)

        @block.scalar
        def _(act):
            def square(N, r):
                s, rows = r % 2, ROWS[r]
                act.wait_ge(x_in[s], (64 if s == 0 else 32) * N + {0: 48, 1: 16, 2: 64, 3: 32}[r])
                need(act, x_lo, 4 * N + r - 1)
                act.activation(ps[0:rows, 4 + 2 * s:6 + 2 * s, :].rearrange("p b t -> p (b t)"),
                               xrow[0:rows, s, :], ACT.Square, scale=RMS_SCALE,
                               accum_out=ssq[0:rows, r:r + 1]).then_inc(x_sumsq, 1)

            def scale(N, r):
                s, rows = r % 2, ROWS[r]
                act.wait_ge(x_rstd, 4 * N + r + 1)
                act.activation(xrow[0:rows, s, :], xrow[0:rows, s, :], ACT.Copy,
                               scale=rstd[0:rows, r:r + 1]).then_inc(x_scaled, 1)

            def high(N, r, q):
                if r == 0:
                    need(act, projected, M * (N - 1))
                act.wait_ge(x_turned, 4 * N + r + 1)
                act.activation(xT[q][:, 0, :, P * r:P * r + ROWS[r]], turned(r)[:, :, 0:ROWS[r]],
                               ACT.Copy).then_inc(x_hi, 1)

            def weight_high(p, m):
                c = M * p + m
                if p < PASSES:
                    act.wait_ge(w_scaled, c + 1)
                else:
                    act.wait_ge(w_in_s[c % 2], 16 * (c // 2 + 1))
                if p:
                    act.wait_ge(projected, M * (BLOCKS * p - 1) + m + 1)
                act.activation(slot(m)[0], raw[:, c % 2, :], ACT.Copy).then_inc(w_hi, 1)

            def evacuate(p, i, n, q, m):
                kind, j = TILES[m]
                e = ACT_TILES.index(m)
                act.wait_ge(projected, M * n + m + 1)
                bank = ps[:, (2 * q + m) % PROJ_BANKS, 0:TB]
                if kind == "g":
                    if j == 0:
                        need(act, gated, gated_count_before(p, i, "u"))
                    else:
                        need(act, outa_out, 32 * n)
                    act.activation(tmp[:, j, :], bank, ACT.Sigmoid).then_inc(act_evac, 1)
                elif kind == "zb":
                    need(act, zb_out, 32 * n + 16 * j)
                    act.activation(szb[:, :], bank, ACT.Silu).then_inc(act_evac, 1)
                elif kind == "h":
                    if j == 0:
                        act.wait_ge(v_ready, v_count(p, i, 0))
                    else:
                        act.wait_ge(gated, gated_count(p, i, 0, "u"))
                    act.activation(tmp[:, 0, :], bank, ACT.Copy).then_inc(act_evac, 1)
                else:
                    if j == 0:
                        act.wait_ge(v_ready, v_count(p, i, 1))
                    else:
                        act.wait_ge(outa_out, 32 * n + 16)
                    act.activation(tmp[:, 1, :], bank, ACT.Silu).then_inc(act_evac, 1)

            extras = {-1: [(square, 0)], 0: [(scale, 0), (square, 1)], 2: [(scale, 1)], 3: [(high, 0)],
                      5: [(high, 1), (square, 2)], 6: [(scale, 2), (square, 3)], 7: [(scale, 3)],
                      9: [(high, 2)], 11: [(high, 3)]}

            def proj_block(p, i, n, q):
                if first(i) and p:
                    for m in range(LEAD):
                        weight_high(p, m)
                for m in range(-1, M):
                    if first(i) and m >= 0 and m + LEAD < M:
                        weight_high(p, m + LEAD)
                    if m in ACT_TILES:
                        evacuate(p, i, n, q, m)
                    if not last(n):
                        for what, r in extras.get(m, []):
                            what(n + 1, r, (q + 1) % 2) if what is high else what(n + 1, r)
                    elif m >= 2 and m - 2 < KC:
                        weight_high(2, m - 2)
            square(0, 0)
            square(0, 1)
            scale(0, 0)
            weight_high(0, 0)
            scale(0, 1)
            high(0, 0, 0)
            square(0, 2)
            high(0, 1, 0)
            square(0, 3)
            scale(0, 2)
            scale(0, 3)
            weight_high(0, 1)
            high(0, 2, 0)
            high(0, 3, 0)
            weight_high(0, 2)
            run_blocks(act, proj_block)

            def mixed_a_high(L, s):
                w = ln_width(L)
                act.wait_ge(ld[s], 24 * (L - s) + 48)
                need(act, out_done, before_rows(L - 1))
                act.activation(MIX[s][:, 0, 0:JT, 0:w], oa[:, s, :, 0:w], ACT.Copy).then_inc(a_hi, 1)

            def squares(L, s):
                w = ln_width(L)
                act.wait_ge(ln, ln_event(L, 3))
                act.activation(tb[:, :, 0:w], cb[:, s, 0:2, 0:w], ACT.Square).then_inc(ln_sq, 1)
                act.wait_ge(ln_mean, L + 1)
                act.activation(ta[:, :, 0:w], cb[:, s, 2:4, 0:w], ACT.Square).then_inc(ln_sq, 1)

            def silus(L, s):
                w = ln_width(L)
                act.wait_ge(ln, ln_event(L, 18))
                for j in range(JT):
                    act.activation(cb[:, s, j, 0:w], cb[:, s, j, 0:w], ACT.Silu, scale=ln_g[:, j:j + 1],
                                   bias=ln_b[:, j:j + 1]).then_inc(ln_silu, 1)

            def mixed_b_high(L, s):
                w = ln_width(L)
                act.wait_ge(ln, ln_event(L, 19))
                act.activation(MIX[s][:, 0, JT:, 0:w], cb[:, s, :, 0:w], ACT.Copy).then_inc(b_hi, 1)

            def row_square(R, s, rows):
                act.wait_ge(h_done, R + 1)
                act.activation(out_pair(s)[0:rows, :], hrow[0:rows, s, :], ACT.Square, scale=RMS_SCALE,
                               accum_out=ssq[0:rows, s:s + 1]).then_inc(h_sumsq, 1)

            def step(L, s):
                tiles = row_tiles(L)
                n1 = not is_last(L)
                if n1:
                    mixed_a_high(L + 1, 1 - s)
                if len(tiles) == 1:
                    row_square(*tiles[0])
                    squares(1, 1)
                    silus(1, 1)
                    mixed_b_high(1, 1)
                    return
                row_square(*tiles[0])
                if n1:
                    squares(L + 1, 1 - s)
                row_square(*tiles[1])
                if n1:
                    silus(L + 1, 1 - s)
                row_square(*tiles[2])
                if n1:
                    mixed_b_high(L + 1, 1 - s)
                row_square(*tiles[3])

            mixed_a_high(0, 0)
            squares(0, 0)
            silus(0, 0)
            mixed_b_high(0, 0)
            run_steps(act, step)

        @block.vector
        def _(dve):
            def low(N, r, q):
                dve.wait_ge(x_hi, 4 * N + r + 1)
                cols = slice(P * r, P * r + ROWS[r])
                dve.tensor_tensor(xT[q][:, 1, :, cols], turned(r)[:, :, 0:ROWS[r]],
                                  xT[q][:, 0, :, cols].bitcast(F32), ALU.subtract).then_inc(x_lo, 1)

            def weight_low(p, m):
                c = M * p + m
                dve.wait_ge(w_hi, c + 1)
                hi, lo = slot(m)
                dve.tensor_tensor(lo, raw[:, c % 2, :], hi.bitcast(F32), ALU.subtract).then_inc(w_lo, 1)

            def window_edges(p, i, n):
                need(dve, taps_done, NT * n)
                if first(i):
                    js = slice(2 * p, 2 * p + 2)
                    need(dve, state_out, 64 * p)
                    dve.tensor_copy(v[:, :, 0:HB], hist_b[:, js, :]).then_inc(edges, 1)
                    dve.memset(v[:, :, HB + SAMPLE:2 * HB + SAMPLE], 0.0).then_inc(edges, 1)
                    dve.tensor_copy(u[:, :, UH0:UH0 + HA], hist_a[:, js, :]).then_inc(edges, 1)
                    dve.memset(u[:, :, UH0 + HA + SAMPLE:P0 + HA], 0.0).then_inc(edges, 1)
                    dve.memset(u[:, :, 0:UH0], 0.0).then_inc(edges, 1)
                else:
                    dve.wait_ge(state_out, 64 * p + 32)
                    dve.tensor_copy(v[:, :, VH:VH + HB], v[:, :, VW - HB:VW]).then_inc(edges, 1)
                    dve.tensor_copy(u[:, :, 0:HA], u[:, :, UW - HA:UW]).then_inc(edges, 1)

            def make_v(p, i, n, q, j):
                if j == 0:
                    dve.wait_ge(edges, edge_count(p, i))
                dve.wait_ge(act_evac, 8 * n + 1 + j)
                dve.wait_ge(projected, M * n + AT["a", j] + 1)
                bank = (2 * q + AT["a", j]) % PROJ_BANKS
                parts = [(HB, S0, SAMPLE), (VH + HB + P0, P0, TB - P0)] if first(i) else [(VH + HB, 0, TB)]
                for at, c, w in parts:
                    dve.tensor_tensor(v[:, j, at:at + w], ps[:, bank, c:c + w], tmp[:, j, c:c + w],
                                      ALU.mult).then_inc(v_ready, 1)

            def tap(p, i, n, x):
                j, k = TAPS[x]
                a, w = (0, ACCW) if first(i) else (AC0, TB)
                window, dst = v[:, j, a + k:a + k + w], acc[:, j, a:a + w]
                jj = 2 * p + j
                if k == 0:
                    if j == 0:
                        need(dve, conv_out, 16 * n)
                        if not first(i) or p:
                            dve.wait_ge(conv_out0, 16 * (p + (not first(i))))
                    dve.wait_ge(v_ready, v_count(p, i, j))
                    dve.tensor_scalar(dst, window, wb[:, jj, 0:1], bias_b[:, jj:jj + 1], ALU.mult,
                                      ALU.add).then_inc(taps_done, 1)
                else:
                    dve.wait_ge(taps_done, NT * n + TAP_AT[j, k - 1] + 1)
                    dve.scalar_tensor_tensor(dst, window, wb[:, jj, k:k + 1], dst, ALU.mult,
                                             ALU.add).then_inc(taps_done, 1)

            def conv_a(p, i, n, q, j):
                dve.wait_ge(act_evac, 8 * n + (5 if j == 0 else 7))
                dve.wait_ge(projected, M * n + AT["c", j] + 1)
                bank = (2 * q + AT["c", j]) % PROJ_BANKS
                parts = [(UH0 + HA, S0, SAMPLE), (HA + P0, P0, TB - P0)] if first(i) else [(HA, 0, TB)]
                need(dve, gated, gated_count(p, i, j, "u", back=len(parts)))
                for at, c, w in parts:
                    dve.tensor_tensor(u[:, j, at:at + w], ps[:, bank, c:c + w], tmp[:, 0, c:c + w],
                                      ALU.mult).then_inc(gated, 1)
                jj = 2 * p + j
                for k in range(KA):
                    dve.wait_ge(gated, gated_count(p, i, j, "taps", back=KA - k))
                    if k == 0:
                        dve.tensor_scalar(ca[:, :], u[:, j, 0:TB], wa[:, jj, 0:1], None,
                                          ALU.mult).then_inc(gated, 1)
                    else:
                        dve.scalar_tensor_tensor(ca[:, :], u[:, j, k:k + TB], wa[:, jj, k:k + 1],
                                                 ca[:, :], ALU.mult, ALU.add).then_inc(gated, 1)

            def halves(i):
                return [(UH0, S0, SAMPLE), (P0, P0, TB - P0)] if first(i) else [(0, 0, TB)]

            def gate_b(p, i, n, q, j):
                dve.wait_ge(projected, M * n + AT["b", j] + 1)
                dve.wait_ge(gated, gated_count(p, i, j, "taps"))
                bank = (2 * q + AT["b", j]) % PROJ_BANKS
                for a, c, w in halves(i):
                    dve.tensor_tensor(ca[:, a:a + w], ps[:, bank, c:c + w], ca[:, a:a + w],
                                      ALU.mult).then_inc(gated, 1)

            def gate_z(p, i, n, q, j):
                dve.wait_ge(act_evac, 8 * n + (6 if j == 0 else 8))
                dve.wait_ge(gated, gated_count(p, i, j, "b"))
                for a, c, w in halves(i):
                    dve.tensor_tensor(tmp[:, 1, c:c + w], ca[:, a:a + w], tmp[:, 1, c:c + w],
                                      ALU.mult).then_inc(gated, 1)

            serve = {AT["a", 0]: (make_v, 0), AT["a", 1]: (make_v, 1), AT["c", 0]: (conv_a, 0),
                     AT["b", 0]: (gate_b, 0), AT["z", 0]: (gate_z, 0), AT["c", 1]: (conv_a, 1),
                     AT["b", 1]: (gate_b, 1), AT["z", 1]: (gate_z, 1)}
            lows = {3: 0, 5: 1, 9: 2, 10: 3}

            def proj_block(p, i, n, q):
                if first(i) and p:
                    for m in range(LEAD):
                        weight_low(p, m)
                done = 0
                window_edges(p, i, n)
                for m in range(M):
                    if first(i) and m + LEAD < M:
                        weight_low(p, m + LEAD)
                    if m in serve:
                        serve[m][0](p, i, n, q, serve[m][1])
                    for x in range(done, TAP_STOPS.get(m, done)):
                        tap(p, i, n, x)
                    done = max(done, TAP_STOPS.get(m, done))
                    if m in lows and not last(n):
                        low(n + 1, lows[m], (q + 1) % 2)
                    if last(n) and m >= 2 and m - 2 < KC:
                        weight_low(2, m - 2)
            low(0, 0, 0)
            low(0, 1, 0)
            weight_low(0, 0)
            weight_low(0, 1)
            low(0, 2, 0)
            low(0, 3, 0)
            weight_low(0, 2)
            dve.wait_ge(const_in, 128)
            run_blocks(dve, proj_block)

            def chained(L, k, instruction):
                need(dve, ln, ln_event(L, k - 1))
                instruction().then_inc(ln, 1)

            def sums(L, s):
                w = ln_width(L)
                dve.wait_ge(ld[s], 24 * (L - s) + 48)
                chained(L, 1, lambda: dve.tensor_tensor(ta[:, :, 0:w], cb[:, s, 0:2, 0:w],
                                                        cb[:, s, 2:4, 0:w], ALU.add))
                chained(L, 2, lambda: dve.tensor_tensor(ta[:, 0, 0:w], ta[:, 0, 0:w], ta[:, 1, 0:w], ALU.add))

            def centre(L, s):
                w = ln_width(L)
                dve.wait_ge(ln_mean, L + 1)
                mean = ps[:, 4, 0:w].unsqueeze(1).to_broadcast([P, JT, w])
                chained(L, 3, lambda: dve.tensor_tensor(cb[:, s, :, 0:w], cb[:, s, :, 0:w], mean, ALU.subtract))

            def square_sums(L, s):
                w = ln_width(L)
                dve.wait_ge(ln_sq, 2 * L + 2)
                chained(L, 4, lambda: dve.tensor_tensor(tb[:, :, 0:w], tb[:, :, 0:w], ta[:, :, 0:w], ALU.add))
                chained(L, 5, lambda: dve.tensor_tensor(tb[:, 0, 0:w], tb[:, 0, 0:w], tb[:, 1, 0:w], ALU.add))

            def normalise(L, s):
                w = ln_width(L)
                var, y, t = ps[:, 5, 0:w], ta[:, 0, 0:w], ta[:, 1, 0:w]
                dve.wait_ge(ln_var, L + 1)
                chained(L, 6, lambda: dve.tensor_scalar(y, var, LN_EPS, None, ALU.add))
                chained(L, 7, lambda: dve.tensor_scalar(y.bitcast(I32), y.bitcast(I32), -0.5, RSQRT_SEED,
                                                        ALU.mult, ALU.add))
                for k in range(3):
                    chained(L, 8 + 3 * k, lambda: dve.scalar_tensor_tensor(t, y, -0.5, y, ALU.mult, ALU.mult))
                    chained(L, 9 + 3 * k, lambda: dve.scalar_tensor_tensor(t, var, LN_EPS, t, ALU.add, ALU.mult))
                    chained(L, 10 + 3 * k, lambda: dve.scalar_tensor_tensor(y, t, 1.5, y, ALU.add, ALU.mult))
                a_low(L, s)
                yb = y.unsqueeze(1).to_broadcast([P, JT, w])
                chained(L, 18, lambda: dve.tensor_tensor(cb[:, s, :, 0:w], cb[:, s, :, 0:w], yb, ALU.mult))

            def a_low(L, s):
                w = ln_width(L)
                dve.wait_ge(a_hi, L + 1)
                chained(L, 17, lambda: dve.tensor_tensor(MIX[s][:, 1, 0:JT, 0:w], oa[:, s, :, 0:w],
                                                         MIX[s][:, 0, 0:JT, 0:w].bitcast(F32), ALU.subtract))

            def gate(L, s):
                w = ln_width(L)
                dve.wait_ge(ln_silu, 4 * L + 4)
                chained(L, 19, lambda: dve.tensor_tensor(cb[:, s, :, 0:w], cb[:, s, :, 0:w],
                                                         zt[:, s, :, 0:w], ALU.mult))

            def b_low(L, s):
                w = ln_width(L)
                dve.wait_ge(b_hi, L + 1)
                chained(L, 20, lambda: dve.tensor_tensor(MIX[s][:, 1, JT:, 0:w], cb[:, s, :, 0:w],
                                                         MIX[s][:, 0, JT:, 0:w].bitcast(F32), ALU.subtract))

            def add_residual(R, s, rows):
                dve.wait_ge(out_done, R + 1)
                dve.wait_ge(res_in[s], 8 * (R - s) + 16)
                need(dve, y_out[s], 8 * (R - s))
                dve.tensor_tensor(hrow[0:rows, s, :], out_pair(s)[0:rows, :], raw[0:rows, s, :],
                                  ALU.add).then_inc(h_done, 1)

            def finish_rows(R, s, rows):
                dve.wait_ge(h_rstd, R + 1)
                dve.scalar_tensor_tensor(hrow[0:rows, s, :], hrow[0:rows, s, :], rstd[0:rows, s:s + 1],
                                         fgain[0:rows, :], ALU.mult, ALU.mult).then_inc(y_done, 1)

            def step(L, s):
                tiles = row_tiles(L)
                n1, o = not is_last(L), 1 - s
                if len(tiles) == 1:
                    sums(1, 1)
                    centre(1, 1)
                    add_residual(*tiles[0])
                    square_sums(1, 1)
                    normalise(1, 1)
                    finish_rows(*tiles[0])
                    gate(1, 1)
                    b_low(1, 1)
                    return
                if n1:
                    sums(L + 1, o)
                add_residual(*tiles[0])
                if n1:
                    centre(L + 1, o)
                finish_rows(*tiles[0])
                if n1:
                    square_sums(L + 1, o)
                add_residual(*tiles[1])
                if n1:
                    normalise(L + 1, o)
                finish_rows(*tiles[1])
                if n1:
                    gate(L + 1, o)
                add_residual(*tiles[2])
                if n1:
                    b_low(L + 1, o)
                finish_rows(*tiles[2])
                add_residual(*tiles[3])
                finish_rows(*tiles[3])

            dve.wait_ge(fg_in, 16)
            sums(0, 0)
            centre(0, 0)
            square_sums(0, 0)
            normalise(0, 0)
            gate(0, 0)
            b_low(0, 0)
            run_steps(dve, step)

        @block.tensor
        def _(pe):
            def split_product(out, terms):
                mm = None
                for x, (ahi, alo, bhi, blo) in enumerate(terms):
                    pe.matmul(out, ahi, bhi, start=(x == 0), stop=False)
                    pe.matmul(out, ahi, blo, start=False, stop=False)
                    mm = pe.matmul(out, alo, bhi, start=False, stop=(x == len(terms) - 1))
                return mm

            def transposes(N, r):
                rows = ROWS[r]
                pe.wait_ge(x_scaled, 4 * N + r + 1)
                for k in range(KC):
                    mm = pe.transpose(turned(r)[:, k, 0:rows], xrow[0:rows, r % 2, P * k:P * (k + 1)],
                                      ident[0:rows, 0:rows])
                mm.then_inc(x_turned, 1)

            def project(p, i, n, q, m):
                if m == 0:
                    pe.wait_ge(x_lo, 4 * n + 4)
                if first(i):
                    pe.wait_ge(w_lo, M * p + m + 1)
                b = (m - PROJ_BANKS) % M
                kind, j = TILES[b]
                if m < PROJ_BANKS:
                    if b in ACT_TILES:
                        need(pe, act_evac, 8 * (n - 1) + ACT_TILES.index(b) + 1)
                    else:
                        need(pe, gated, gated_count_before(p, i, "u" if kind == "c" else "b"))
                elif b in ACT_TILES:
                    pe.wait_ge(act_evac, 8 * n + ACT_TILES.index(b) + 1)
                elif kind == "a":
                    pe.wait_ge(v_ready, v_count(p, i, j))
                else:
                    pe.wait_ge(gated, gated_count(p, i, j, "u" if kind == "c" else "b"))
                hi, lo = slot(m)
                x = xT[q]
                split_product(ps[:, (2 * q + m) % PROJ_BANKS, 0:TB],
                              [(hi[:, P * k:P * (k + 1)], lo[:, P * k:P * (k + 1)], x[:, 0, k, :], x[:, 1, k, :])
                               for k in range(KC)]).then_inc(projected, 1)

            def proj_block(p, i, n, q):
                for m in range(M):
                    if m in TRANSPOSE_AT and not last(n):
                        transposes(n + 1, TRANSPOSE_AT[m])
                    project(p, i, n, q, m)

            pe.wait_ge(ready0, 5)
            for r in range(4):
                transposes(0, r)
            run_blocks(pe, proj_block)

            def channel_mean(L, dst, src, count, done):
                w = ln_width(L)
                pe.wait_ge(ln, count)
                pe.matmul(dst[:, 0:w], mean_w[:, :], src[:, 0:w], start=True, stop=True).then_inc(done, 1)

            def mean(L):
                channel_mean(L, ps[:, 4, :], ta[:, 0, :], ln_event(L, 2), ln_mean)

            def var(L):
                channel_mean(L, ps[:, 5, :], tb[:, 0, :], ln_event(L, 5), ln_var)

            def rows_out(L, s, r, R, rs):
                pe.wait_ge(ln, ln_event(L, LN_OPS))
                need(pe, h_sumsq, R - 1)
                mx = MIX[s]
                for half_d in range(2):
                    cols = slice(512 * half_d, 512 * half_d + 512)
                    terms = []
                    for e in range(KC):
                        hi, lo = slot(e)
                        terms.append((mx[:, 0, e, P * r:P * (r + 1)], mx[:, 1, e, P * r:P * (r + 1)],
                                      hi[:, cols], lo[:, cols]))
                    mm = split_product(ps[:, 2 * rs + half_d, :], terms)
                mm.then_inc(out_done, 1)

            def step(L, s):
                n1 = not is_last(L)
                tiles = row_tiles(L)
                if len(tiles) == 1:
                    mean(1)
                    rows_out(L, s, 0, 0, 0)
                    var(1)
                    return
                for r, (R, rs, _) in enumerate(tiles):
                    rows_out(L, s, r, R, rs)
                    if n1 and r == 0:
                        mean(L + 1)
                    if n1 and r == 1:
                        var(L + 1)

            pe.wait_ge(act_evac, 8 * (LAST + 1))
            pe.wait_ge(gated, gated_count(1, BLOCKS - 1, 1, "out"))
            pe.wait_ge(w_lo, M * PASSES + KC)
            mean(0)
            var(0)
            run_steps(pe, step)


def kernel(**inputs):
    import numpy as _np
    import concourse.bacc as _bacc
    from concourse import mybir as _mybir
    from concourse.bass_utils import run_bass_kernel_spmd as _run

    c = _np.ascontiguousarray
    g = {k: _np.asarray(a) for k, a in inputs.items()}
    n_tiles = g["w_in"].shape[2] // P
    by_tile = lambda a: c(a.reshape(-1, P).T)
    arrays = {
        "x_prompt": c(g["x_prompt"][0]),
        "x_sample": c(g["x_sample"][0]),
        "state_conv_a": c(g["state_conv_a"][0, 0].T),
        "state_conv_b": c(g["state_conv_b"][0, 0].T),
        "norm_g": by_tile(g["norm_g"][0]),
        "w_in": c(g["w_in"][0].reshape(KC, P, n_tiles, P).transpose(2, 1, 0, 3)).reshape(n_tiles, P, D),
        "conv_a_w": c(g["conv_a_w"][0].T),
        "conv_b_w": c(g["conv_b_w"][0].T),
        "conv_b_bias": by_tile(g["conv_b_bias"][0]),
        "ln_b_g": by_tile(g["ln_b_g"][0]),
        "ln_b_b": by_tile(g["ln_b_b"][0]),
        "w_out": c(g["w_out"][0]),
        "final_norm_g": c(g["final_norm_g"][None, :]),
    }
    outs = {
        "y_prompt": (SEQ, D), "y_sample": (SAMPLE, D),
        "new_a_prompt": (DA, HA), "new_b_prompt": (DA, HB),
        "new_a_sample": (DA, HA), "new_b_sample": (DA, HB),
    }
    nc = _bacc.Bacc("TRN2", target_bir_lowering=False, num_devices=1)
    A, feed = {}, {}
    for name, a in arrays.items():
        feed[f"in_{name}"] = a
        A[name] = nc.dram_tensor(f"in_{name}", a.shape, _mybir.dt.from_np(a.dtype), kind="ExternalInput").ap()
    for name, shape in outs.items():
        A[name] = nc.dram_tensor(f"out_{name}", shape, F32, kind="ExternalOutput").ap()
    build_program(nc, A)
    r = _run(nc, [feed], core_ids=[0]).results[0]
    state = lambda name: c(r[f"out_{name}"].T)[None, None]
    return (r["out_y_prompt"][None], r["out_y_sample"][None], state("new_a_prompt"), state("new_b_prompt"),
            state("new_a_sample"), state("new_b_sample"))
```

```python
import concourse.bass as bass
from concourse import mybir
from contextlib import ExitStack

F32 = mybir.dt.float32
F32R = mybir.dt.float32r
I32 = mybir.dt.int32
ALU = mybir.AluOpType
ACT = mybir.ActivationFunctionType

P = 128
D = 1024
KC = D // P
DA = 512
JT = DA // P
SEQ, SAMPLE = 4096, 32
KA, KB = 3, 31
HA, HB = KA - 1, KB - 1
RMS_EPS, LN_EPS = 1e-6, 1e-5
RMS_SCALE = D ** -0.5

PASSES = 2
BLOCKS = 9
TB = 460
PAD = BLOCKS * TB - SEQ - SAMPLE
S0, P0 = PAD, PAD + SAMPLE
TOK = BLOCKS * TB
ROWS = [P, P, P, TB - 3 * P]

VW = HB + SAMPLE + HB + (TB - P0)
VH = VW - TB - HB
UW = HA + TB
UH0 = UW - (HA + SAMPLE + HA + TB - P0)
ACCW = VW - HB
AC0 = ACCW - TB

TILES = [("g", 0), ("a", 0), ("g", 1), ("a", 1), ("zb", 0), ("zb", 1), ("h", 0), ("c", 0),
         ("b", 0), ("z", 0), ("h", 1), ("c", 1), ("b", 1), ("z", 1)]
SECTION = {"h": 0, "b": 1, "c": 2, "z": 3, "a": 4, "g": 5, "zb": 6}
M = len(TILES)
AT = {t: m for m, t in enumerate(TILES)}
ACT_TILES = [m for m, (k, _) in enumerate(TILES) if k in ("g", "zb", "h", "z")]
PROJ_BANKS = 4
SLOT = 2 * D
LEAD = 3
EARLY = 8


def splits_at(p, i, m):
    if not isinstance(i, int):
        return None
    if p == 0 and i == 0:
        return (0, m + LEAD) if 0 <= m and m + LEAD < M else None
    if i == 0:
        return (p, EARLY + m) if 0 <= m and EARLY + m < M else None
    if i == BLOCKS - 1:
        return (p + 1, m - 2) if 2 <= m < 2 + EARLY else None
    return None


LN_AT = {"centre": 3, "square_sums": 5, "normalise": 6, "gate": 12}
TAPS = [(0, k) for k in range(13)]
_a, _b = [(1, k) for k in range(KB)], [(0, k) for k in range(13, KB)]
for _k in range(KB):
    TAPS.append(_a[_k])
    if _k < len(_b):
        TAPS.append(_b[_k])
NT = len(TAPS)
TAP_AT = {t: x for x, t in enumerate(TAPS)}
TAP_STOPS = {1: 13, 3: 28, 5: 39, 8: 45, 9: 57, 12: NT}
RSTD_AT = {-1: (0,), 1: (1,), 5: (2,), 6: (3,)}
LOAD_X_AT = {-1: (0, 1), 3: (2,), 5: (3,)}
TRANSPOSE_AT = {3: 0, 5: 1, 9: 2, 11: 3}

OB = 512
RT = OB // P
OBLOCKS = SEQ // OB
LN_OPS = 17
SAMPLE_ROWS = SEQ // P
RSQRT_SEED = 1597463007.0


def build_program(nc, A):
    ctx = ExitStack()
    with ctx:
        def sb(name, shape, dt=F32, scope=ctx):
            return scope.enter_context(nc.sbuf_tensor(name, shape, dt))

        def sb_two(name, shape, scope=ctx):
            with ExitStack() as short:
                split = sb(name, shape, F32R, short)
            return split, sb(f"{name}_f32", shape, F32, scope)

        def sem(name):
            return ctx.enter_context(nc.semaphore(name))

        conv_d = nc.dram_tensor("conv_spill", [DA, TOK], F32).ap()
        zb_d = nc.dram_tensor("zb_spill", [DA, TOK], F32).ap()
        outa_d = nc.dram_tensor("outa_spill", [DA, TOK], F32).ap()

        W, W_f32 = sb_two("w_split", [P, 12 * SLOT])
        raw = sb("w_raw", [P, 2, D])
        ident = sb("ident", [P, P])
        mean_w = sb("mean_w", [P, P])
        gain = sb("gain", [P, KC])
        wb = sb("conv_b_taps", [P, JT, KB])
        bias_b = sb("conv_b_bias_sb", [P, JT])
        wa = sb("conv_a_taps", [P, JT, KA])
        hist_b = sb("hist_b", [P, JT, HB])
        hist_a = sb("hist_a", [P, JT, HA])
        ln_g = sb("ln_g", [P, JT])
        ln_b = sb("ln_b", [P, JT])
        minus_half = sb("minus_half", [P, 1])
        eps = sb("rms_eps", [P, 1])
        ssq = sb("row_mean_sq", [P, 4])
        mean_sq = sb("row_mean_sq_eps", [P, 4])
        rstd = sb("rstd", [P, 4])
        early = ExitStack()
        xT0 = sb("xT0", [P, 2, KC, TB], F32R, early)
        xrow = sb("x_rows", [P, 2, D], F32, early)
        W2, W2_f32 = sb_two("w_split_2", [P, 2 * SLOT], early)
        xT = [xT0, sb("xT1", [P, 2, KC, TB], F32R, early)]
        v = sb("v", [P, 2, VW], F32, early)
        u = sb("u", [P, 2, UW], F32, early)
        tmp = sb("gates", [P, 2, TB], F32, early)
        acc = sb("conv_b_acc", [P, 2, ACCW], F32, early)
        szb = sb("szb", [P, TB], F32, early)
        ca = sb("conv_a_acc", [P, TB], F32, early)
        early.close()
        cb = [sb(f"conv_b_{s}", [P, JT, OB]) for s in range(2)]
        fgain = sb("final_gain", [P, D])
        hrow = sb("h_rows", [P, 2, D])
        sb("gap", [P, 2 * KC * TB - 2 * JT * OB - 3 * D])
        ta = sb("ln_tmp_a", [P, 2, OB])
        tb = sb("ln_tmp_b", [P, 2, OB])
        mix2, mix2_f32 = sb_two("mixed_1", [P, 2, 2 * JT, OB])

        def slot(m):
            t, n = (W, m) if m < 12 else (W2, m - 12)
            return t[:, n * SLOT:n * SLOT + D], t[:, n * SLOT + D:(n + 1) * SLOT]

        mix1, mix1_f32 = (t[:, 8 * SLOT:12 * SLOT].rearrange("p (l e t) -> p l e t", l=2, t=OB)
                          for t in (W, W_f32))
        MIX = [mix1, mix2[:, :, :, :]]
        MIX_F32 = [mix1_f32, mix2_f32[:, :, :, :]]

        ps = ctx.enter_context(nc.psum_tensor("ps", [P, 8, 512], F32))

        def starts(N):
            return isinstance(N, int) and N == 0

        def banks(N, r):
            b = 2 * (r % 2) + (0 if starts(N) and r >= 2 else 4)
            return ps[:, b:b + 2, :]

        def turned(N, r):
            return banks(N, r).rearrange("p b (c t) -> p (b c) t", t=P)

        def rows_at(N, r):
            if starts(N) and r >= 2:
                return W2_f32[:, D * (r - 2):D * (r - 1)]
            return xrow[:, r % 2, :]

        def out_pair(s):
            return ps[:, 2 * s:2 * s + 2, :].rearrange("p b t -> p (b t)")

        const_in = sem("const_in")
        ready0 = sem("pool_consts_ready")
        gain_in = sem("norm_g_in")
        x_in = [sem(f"x_rows_in_{s}") for s in range(2)]
        x_in0 = [sem(f"x_rows_in_first_{r}") for r in (2, 3)]
        x_sumsq = sem("x_sumsq")
        x_ms = sem("x_mean_square")
        x_rstd = sem("x_rstd")
        x_scaled = sem("x_scaled")
        x_turned = sem("x_turned")
        x_hi = sem("x_hi")
        x_lo = sem("x_lo")
        w_in_s = [sem(f"w_raw_in_{s}") for s in range(2)]
        w_scaled = sem("w_scaled")
        w_hi = sem("w_hi")
        w_lo = sem("w_lo")
        projected = sem("projected")
        act_evac = sem("act_evacuated")
        edges = sem("window_edges")
        v_ready = sem("v_ready")
        taps_done = sem("taps_done")
        gated = sem("gated_steps")
        conv_out = sem("conv_out")
        conv_out0 = sem("conv_out_sample")
        zb_out = sem("zb_out")
        outa_out = sem("outa_out")
        state_out = sem("state_out")
        fg_in = sem("final_gain_in")
        cb_in = [sem(f"conv_b_in_{s}") for s in range(2)]
        zt_in = [sem(f"silu_zb_in_{s}") for s in range(2)]
        oa_in = [sem(f"out_a_in_{s}") for s in range(2)]
        ln_sum = sem("ln_sums")
        ln = sem("ln_steps")
        ln_mean = sem("ln_mean")
        ln_sq = sem("ln_squares")
        ln_var = sem("ln_var")
        ln_silu = sem("ln_silu")
        a_hi = sem("mixed_a_hi")
        a_lo = sem("mixed_a_lo")
        b_hi = sem("mixed_b_hi")
        out_done = sem("rows_multiplied")
        res_in = [sem(f"residual_in_{s}") for s in range(2)]
        h_done = sem("h_done")
        h_sumsq = sem("h_sumsq")
        h_ms = sem("h_mean_square")
        h_rstd = sem("h_rstd")
        y_done = sem("y_done")
        y_out = [sem(f"y_out_{s}") for s in range(2)]

        def need(eng, s, value):
            if not (isinstance(value, int) and value <= 0):
                eng.wait_ge(s, value)

        def v_count(p, i, j):
            return 20 * p + 2 * (j + 1) if first(i) else 20 * p + 3 + 2 * i + j

        STEP = {"u": (2, 1), "taps": (5, 4), "b": (7, 5), "out": (9, 6)}

        def gated_count(p, i, j, what, back=0):
            if first(i):
                return 114 * p + 9 * j + STEP[what][0] - back
            return 114 * p + 6 + 12 * i + 6 * j + STEP[what][1] - back

        def gated_count_before(p, i, what):
            if first(i):
                return gated_count(p - 1, BLOCKS - 1, 1, what) if p else 0
            return 114 * p + 12 * i + STEP[what][1]

        def edge_count(p, i):
            return 21 * p + 5 if first(i) else 21 * p + 5 + 2 * i

        def first(i):
            return isinstance(i, int) and i == 0

        def run_blocks(eng, block):
            for p in range(PASSES):
                block(p, 0, BLOCKS * p, p)
                pairs = (BLOCKS - 1) // 2 - 1
                with eng.Fori(0, pairs) as it:
                    for o in range(2):
                        i = 2 * it + (1 + o)
                        block(p, i, i + BLOCKS * p, (BLOCKS * p + 1 + o) % 2)
                for i in range(1 + 2 * pairs, BLOCKS):
                    block(p, i, i + BLOCKS * p, (BLOCKS * p + i) % 2)

        LAST = PASSES * BLOCKS - 1

        def last(n):
            return isinstance(n, int) and n == LAST

        def ln_cols(L):
            return S0 if is_last(L) else P0 + L * OB

        def ln_width(L):
            return P if is_last(L) else OB

        def run_steps(eng, step):
            for L in (0, 1):
                step(L, L % 2)
            with eng.Fori(0, (OBLOCKS - 4) // 2) as it:
                for o in range(2):
                    step(2 * it + (2 + o), o)
            for L in range(OBLOCKS - 2, OBLOCKS + 1):
                step(L, L % 2)

        def row_tiles(L):
            if is_last(L):
                return [(SAMPLE_ROWS, 0, SAMPLE)]
            return [(RT * L + r, r % 2, P) for r in range(RT)]

        def more(L, ahead):
            return not (isinstance(L, int) and L + ahead > OBLOCKS)

        def is_last(L):
            return isinstance(L, int) and L == OBLOCKS

        def ln_event(L, k):
            return LN_OPS * L + k

        block = ctx.enter_context(nc.Block())

        @block.sync
        def _(sp):
            chan = lambda t: t.rearrange("(j p) k -> p j k", p=P)
            consts = [(wb[:, :, :], chan(A["conv_b_w"])), (wa[:, :, :], chan(A["conv_a_w"])),
                      (hist_b[:, :, :], chan(A["state_conv_b"])), (hist_a[:, :, :], chan(A["state_conv_a"])),
                      (bias_b[:, :], A["conv_b_bias"]),
                      (ln_g[:, :], A["ln_b_g"]), (ln_b[:, :], A["ln_b_b"])]

            def load_x(N, i, r):
                s = r % 2
                if starts(N) and r >= 2:
                    src = A["x_prompt"][P * r - P0:P * r - P0 + ROWS[r], :]
                    sp.dma_start(rows_at(N, r)[0:ROWS[r], :], src).then_inc(x_in0[r - 2], 16)
                    return
                need(sp, x_turned, 4 * N + r - 1)
                if r == 0:
                    cuts = [0, S0, P0, P]
                    for a, b in zip(cuts, cuts[1:]):
                        if first(i) and a < P0:
                            src = A["x_sample"][0:b - a, :]
                        else:
                            src = A["x_prompt"][bass.ds(TB * i - P0 + a, b - a), :]
                        sp.dma_start(xrow[a:b, s, :], src).then_inc(x_in[s], 16)
                else:
                    src = A["x_prompt"][bass.ds(TB * i - P0 + P * r, ROWS[r]), :]
                    sp.dma_start(xrow[0:ROWS[r], s, :], src).then_inc(x_in[s], 16)

            def load_w(p, m):
                c = M * p + m
                need(sp, w_lo, c - 1)
                if p < PASSES:
                    k, j = TILES[m]
                    src = A["w_in"][SECTION[k] * JT + 2 * p + j]
                else:
                    src = A["w_out"][P * m:P * (m + 1), :]
                sp.dma_start(raw[:, c % 2, :], src).then_inc(w_in_s[c % 2], 16)

            def spill(dram, p, j, nj=1):
                return dram[P * (2 * p + j):P * (2 * p + j + nj), :].rearrange("(j p) t -> p j t", p=P)

            def store_conv(p, i, n):
                sp.wait_ge(taps_done, NT * n + NT)
                dst = spill(conv_d, p, 0, 2)
                if first(i):
                    sp.dma_start(dst[:, :, S0:P0], acc[:, :, 0:SAMPLE]).then_inc(conv_out0, 16)
                    sp.dma_start(dst[:, :, P0:TB], acc[:, :, AC0 + P0:]).then_inc(conv_out, 16)
                else:
                    sp.dma_start(dst[:, :, bass.ds(TB * i, TB)], acc[:, :, AC0:]).then_inc(conv_out, 16)

            def store_zb(p, i, n, j):
                sp.wait_ge(act_evac, 8 * n + 3 + j)
                sp.dma_start(spill(zb_d, p, j)[:, 0, bass.ds(TB * i, TB)], szb[:, :]).then_inc(zb_out, 16)

            def store_outa(p, i, n, j):
                sp.wait_ge(gated, gated_count(p, i, j, "out"))
                sp.dma_start(spill(outa_d, p, j)[:, 0, bass.ds(TB * i, TB)], tmp[:, 1, :]).then_inc(outa_out, 16)

            def store_states(p, i, kind):
                vs, us = (HB + SAMPLE - HB, UH0 + SAMPLE) if kind == "sample" else (VW - HB, UW - HA)
                sp.wait_ge(v_ready, v_count(p, i, 1))
                sp.dma_start(spill(A[f"new_b_{kind}"], p, 0, 2), v[:, :, vs:vs + HB]).then_inc(state_out, 16)
                sp.wait_ge(gated, gated_count(p, i, 1, "u"))
                sp.dma_start(spill(A[f"new_a_{kind}"], p, 0, 2), u[:, :, us:us + HA]).then_inc(state_out, 16)

            def load_cb(L, s):
                if not isinstance(L, int) or L >= 2:
                    sp.wait_ge(ln, ln_event(L - 2, LN_OPS))
                w = ln_width(L)
                src = conv_d.rearrange("(j p) t -> p j t", p=P)[:, :, bass.ds(ln_cols(L), w)]
                sp.dma_start(cb[s][:, :, 0:w], src).then_inc(cb_in[s], 16)

            def load_mix(L, s):
                if not isinstance(L, int) or L >= 2:
                    sp.wait_ge(out_done, RT * (L - 1))
                w = ln_width(L)
                for at, dram, arrived in ((0, outa_d, oa_in), (JT, zb_d, zt_in)):
                    if isinstance(L, int) and L == 0:
                        sp.wait_ge(projected, M * LAST + (9 if at == 0 else 10))
                    src = dram.rearrange("(j p) t -> p j t", p=P)[:, :, bass.ds(ln_cols(L), w)]
                    sp.dma_start(MIX_F32[s][:, 0, at:at + JT, 0:w], src).then_inc(arrived[s], 16)

            def proj_block(p, i, n, q):
                nxt = i + 1 if not isinstance(i, int) else (i + 1) % BLOCKS
                for m in range(-1, M):
                    w = splits_at(p, i, m + 1)
                    if w:
                        load_w(*w)
                    if m in LOAD_X_AT and not last(n):
                        for r in LOAD_X_AT[m]:
                            load_x(n + 1, nxt, r)
                    if m == 1 and not first(i):
                        store_conv(p, i - 1, n - 1)
                    if m == -1 and last(n):
                        sp.wait_ge(projected, M * LAST)
                        sp.wait_ge(conv_out, 16 * (LAST - 1))
                        sp.wait_ge(conv_out0, 16 * PASSES)
                        load_cb(0, 0)
                    if m == 3 and last(n):
                        load_cb(1, 1)
                        sp.dma_start(fgain[:, :], A["final_norm_g"].to_broadcast([P, D])).then_inc(fg_in, 16)
                    if m == AT["z", 0] and last(n):
                        sp.wait_ge(zb_out, 32 * (LAST + 1))
                        sp.wait_ge(outa_out, 32 * LAST)
                        load_mix(0, 0)
                    if m in (AT["zb", 0], AT["zb", 1]):
                        store_zb(p, i, n, m - AT["zb", 0])
                    if m in (AT["z", 0], AT["z", 1]):
                        store_outa(p, i, n, int(m == AT["z", 1]))
                if first(i):
                    store_states(p, i, "sample")
                if isinstance(i, int) and i == BLOCKS - 1:
                    store_states(p, i, "prompt")
                    store_conv(p, i, n)

            def blocks():
                for p in range(PASSES):
                    proj_block(p, 0, BLOCKS * p, None)
                    proj_block(p, 1, BLOCKS * p + 1, None)
                    with sp.Fori(2, BLOCKS - 1) as i:
                        proj_block(p, i, i + BLOCKS * p, None)
                    proj_block(p, BLOCKS - 1, BLOCKS * p + BLOCKS - 1, None)

            load_x(0, 0, 0)
            load_w(0, 0)
            load_x(0, 0, 1)
            sp.dma_start(gain[:, :], A["norm_g"]).then_inc(gain_in, 16)
            load_x(0, 0, 2)
            load_x(0, 0, 3)
            load_w(0, 1)
            for dst, src in consts:
                sp.dma_start(dst, src).then_inc(const_in, 16)
            load_w(0, 2)
            blocks()

            def rows_of(R, name):
                if isinstance(R, int) and R == SAMPLE_ROWS:
                    return A[f"{name}_sample"]
                return A[f"{name}_prompt"][bass.ds(P * R, P), :]

            def load_residual(R, s, rows):
                need(sp, h_done, R - 1)
                src = rows_of(R, "x")
                sp.dma_start(raw[0:rows, s, :], src).then_inc(res_in[s], 16)

            def store_y(R, s, rows):
                sp.wait_ge(y_done, R + 1)
                sp.dma_start(rows_of(R, "y"), hrow[0:rows, s, :]).then_inc(y_out[s], 16)

            def step(L, s):
                if more(L, 2):
                    load_cb(L + 2, s)
                for r, (R, rs, rows) in enumerate(row_tiles(L)):
                    if not is_last(L):
                        sample = isinstance(R, int) and R + 1 == SAMPLE_ROWS
                        load_residual(R + 1, (rs + 1) % 2, SAMPLE if sample else P)
                    if r == RT - 1 and more(L, 2):
                        load_mix(L + 2, s)
                    store_y(R, rs, rows)

            sp.wait_ge(w_lo, M * PASSES + KC)
            load_residual(0, 0, P)
            sp.wait_ge(projected, M * (LAST + 1))
            sp.wait_ge(outa_out, 32 * (LAST + 1))
            load_mix(1, 1)
            sp.wait_ge(conv_out, 16 * (LAST + 1))
            sp.wait_ge(state_out, 64 * PASSES)
            run_steps(sp, step)
            sp.wait_ge(y_out[0], 16 * (SEQ // P // 2 + 1))
            sp.wait_ge(y_out[1], 16 * (SEQ // P // 2))

        @block.gpsimd
        def _(pool):
            pool.memset(ident[:, :], 0.0).then_inc(ready0, 1)
            pool.memset(mean_w[:, :], 1.0 / DA).then_inc(ready0, 1)
            pool.memset(minus_half[:, :], -0.5).then_inc(ready0, 1)
            pool.memset(eps[:, :], RMS_EPS).then_inc(ready0, 1)
            pool.wait_ge(ready0, 4)
            pool.affine_select(out=ident[:, :], in_=ident[:, :], compare_op=ALU.not_equal, fill=1.0,
                               base=0, pattern=[[-1, P]], channel_multiplier=1).then_inc(ready0, 1)

            def row_rstd(r, rows, sumsq, ms, done, count):
                pool.wait_ge(sumsq, count)
                pool.tensor_tensor(mean_sq[0:rows, r:r + 1], ssq[0:rows, r:r + 1], eps[0:rows, :],
                                   ALU.add).then_inc(ms, 1)
                pool.wait_ge(ms, count)
                pool.tensor_tensor(rstd[0:rows, r:r + 1], mean_sq[0:rows, r:r + 1],
                                   minus_half[0:rows, :], ALU.pow).then_inc(done, 1)

            def scale_w(p, m):
                c = M * p + m
                pool.wait_ge(w_in_s[c % 2], 16 * (c // 2 + 1))
                w = raw[:, c % 2, :].rearrange("p (k c) -> p k c", k=KC)
                pool.tensor_tensor(w, w, gain[:, :].unsqueeze(2).to_broadcast([P, KC, P]),
                                   ALU.mult).then_inc(w_scaled, 1)

            def weight_low(m):
                c = M * PASSES + m
                pool.wait_ge(w_hi, c + 1)
                hi, lo = slot(m)
                pool.tensor_tensor(lo, raw[:, c % 2, :], hi.bitcast(F32), ALU.subtract).then_inc(w_lo, 1)

            def sums(L, s):
                w = ln_width(L)
                pool.wait_ge(cb_in[s], 8 * (L - s) + 16)
                if not isinstance(L, int) or L >= 1:
                    pool.wait_ge(ln, ln_event(L - 1, 15))
                pool.tensor_tensor(ta[:, :, 0:w], cb[s][:, 0:2, 0:w], cb[s][:, 2:4, 0:w],
                                   ALU.add).then_inc(ln_sum, 1)
                pool.wait_ge(ln_sum, 2 * L + 1)
                pool.tensor_tensor(ta[:, 0, 0:w], ta[:, 0, 0:w], ta[:, 1, 0:w], ALU.add).then_inc(ln_sum, 1)

            def a_low(L, s):
                w = ln_width(L)
                pool.wait_ge(a_hi, L + 1)
                pool.tensor_tensor(MIX[s][:, 0, 0:JT, 0:w], MIX_F32[s][:, 0, 0:JT, 0:w], MIX[s][:, 1, 0:JT, 0:w].bitcast(F32),
                                   ALU.subtract).then_inc(a_lo, 1)

            def proj_block(p, i, n, q):
                for m in range(-1, M):
                    w = splits_at(p, i, m + 1)
                    if w and w[0] < PASSES:
                        scale_w(*w)
                    w = splits_at(p, i, m)
                    if w and w[0] == PASSES:
                        weight_low(w[1])
                    if m in RSTD_AT and not last(n):
                        for r in RSTD_AT[m]:
                            row_rstd(r, ROWS[r], x_sumsq, x_ms, x_rstd, 4 * n + 5 + r)
                    if last(n) and m == 1:
                        sums(0, 0)
                    if last(n) and m == M - 4:
                        sums(1, 1)
                    if last(n) and m == M - 2:
                        a_low(0, 0)

            row_rstd(0, P, x_sumsq, x_ms, x_rstd, 1)
            row_rstd(1, P, x_sumsq, x_ms, x_rstd, 2)
            row_rstd(2, P, x_sumsq, x_ms, x_rstd, 3)
            pool.wait_ge(gain_in, 16)
            row_rstd(3, ROWS[3], x_sumsq, x_ms, x_rstd, 4)
            for m in range(LEAD):
                scale_w(0, m)
            for p in range(PASSES):
                proj_block(p, 0, BLOCKS * p, None)
                with pool.Fori(1, BLOCKS - 1) as i:
                    proj_block(p, i, i + BLOCKS * p, None)
                proj_block(p, BLOCKS - 1, BLOCKS * p + BLOCKS - 1, None)

            def step(L, s):
                for r, (R, rs, rows) in enumerate(row_tiles(L)):
                    row_rstd(rs, rows, h_sumsq, h_ms, h_rstd, R + 1)
                    if r == 0 and more(L, 1):
                        a_low(L + 1, 1 - s)
                    if r == 2 and more(L, 2):
                        sums(L + 2, s)

            run_steps(pool, step)

        @block.scalar
        def _(act):
            def square(N, r):
                s, rows = r % 2, ROWS[r]
                if starts(N):
                    act.wait_ge(x_in[r] if r < 2 else x_in0[r - 2], 48 if r == 0 else 16)
                else:
                    act.wait_ge(x_in[s], (64 if s == 0 else 32) * N + {0: 32, 1: 0, 2: 48, 3: 16}[r])
                    act.wait_ge(x_lo, 4 * N + r - 1)
                act.activation(banks(N, r)[0:rows, :, :].rearrange("p b t -> p (b t)"),
                               rows_at(N, r)[0:rows, :], ACT.Square, scale=RMS_SCALE,
                               accum_out=ssq[0:rows, r:r + 1]).then_inc(x_sumsq, 1)

            def scale(N, r):
                s, rows = r % 2, ROWS[r]
                act.wait_ge(x_rstd, 4 * N + r + 1)
                act.activation(xrow[0:rows, s, :], xrow[0:rows, s, :], ACT.Copy,
                               scale=rstd[0:rows, r:r + 1]).then_inc(x_scaled, 1)

            def high(N, r, q):
                if r == 0:
                    need(act, projected, M * (N - 1))
                act.wait_ge(x_turned, 4 * N + r + 1)
                act.activation(xT[q][:, 0, :, P * r:P * r + ROWS[r]], turned(N, r)[:, :, 0:ROWS[r]],
                               ACT.Copy).then_inc(x_hi, 1)

            def weight_high(p, m):
                c = M * p + m
                if p < PASSES:
                    act.wait_ge(w_scaled, c + 1)
                else:
                    act.wait_ge(w_in_s[c % 2], 16 * (c // 2 + 1))
                if p:
                    act.wait_ge(projected, M * (BLOCKS * p - 1) + m + 1)
                act.activation(slot(m)[0], raw[:, c % 2, :], ACT.Copy).then_inc(w_hi, 1)

            def evacuate(p, i, n, q, m):
                kind, j = TILES[m]
                e = ACT_TILES.index(m)
                act.wait_ge(projected, M * n + m + 1)
                bank = ps[:, (2 * q + m) % PROJ_BANKS, 0:TB]
                if kind == "g":
                    if j == 0:
                        need(act, gated, gated_count_before(p, i, "u"))
                    else:
                        need(act, outa_out, 32 * n)
                    act.activation(tmp[:, j, :], bank, ACT.Sigmoid).then_inc(act_evac, 1)
                elif kind == "zb":
                    need(act, zb_out, 32 * n + 16 * j)
                    act.activation(szb[:, :], bank, ACT.Silu).then_inc(act_evac, 1)
                elif kind == "h":
                    if j == 0:
                        act.wait_ge(v_ready, v_count(p, i, 0))
                    else:
                        act.wait_ge(gated, gated_count(p, i, 0, "u"))
                    act.activation(tmp[:, 0, :], bank, ACT.Copy).then_inc(act_evac, 1)
                else:
                    if j == 0:
                        act.wait_ge(v_ready, v_count(p, i, 1))
                    else:
                        act.wait_ge(outa_out, 32 * n + 16)
                    act.activation(tmp[:, 1, :], bank, ACT.Silu).then_inc(act_evac, 1)

            extras = {-1: [(square, 0)], 0: [(scale, 0), (square, 1)], 2: [(scale, 1)], 3: [(high, 0)],
                      5: [(high, 1), (square, 2)], 6: [(scale, 2), (square, 3)], 7: [(scale, 3)],
                      9: [(high, 2)], 11: [(high, 3)]}

            def mixed_a_high(L, s):
                w = ln_width(L)
                act.wait_ge(oa_in[s], 8 * (L - s) + 16)
                if isinstance(L, int) and L == 0:
                    act.wait_ge(projected, M * LAST + 11)
                act.activation(MIX[s][:, 1, 0:JT, 0:w], MIX_F32[s][:, 0, 0:JT, 0:w],
                               ACT.Copy).then_inc(a_hi, 1)

            def squares(L, s):
                w = ln_width(L)
                act.wait_ge(ln, ln_event(L, 1))
                act.activation(tb[:, :, 0:w], cb[s][:, 0:2, 0:w], ACT.Square).then_inc(ln_sq, 1)
                act.wait_ge(ln_mean, L + 1)
                act.activation(ta[:, :, 0:w], cb[s][:, 2:4, 0:w], ACT.Square).then_inc(ln_sq, 1)

            def silus(L, s):
                w = ln_width(L)
                act.wait_ge(ln, ln_event(L, 15))
                for j in range(JT):
                    act.activation(cb[s][:, j, 0:w], cb[s][:, j, 0:w], ACT.Silu, scale=ln_g[:, j:j + 1],
                                   bias=ln_b[:, j:j + 1]).then_inc(ln_silu, 1)

            def mixed_b_high(L, s):
                w = ln_width(L)
                act.wait_ge(ln, ln_event(L, 16))
                if isinstance(L, int) and L == 0:
                    act.wait_ge(projected, M * LAST + 12)
                act.activation(MIX[s][:, 1, JT:, 0:w], cb[s][:, :, 0:w], ACT.Copy).then_inc(b_hi, 1)

            first_ln = {LN_AT["centre"]: [squares], LN_AT["normalise"] + 2: [silus],
                        M - 3: [mixed_a_high], M - 2: [mixed_b_high]}

            def proj_block(p, i, n, q):
                for m in range(-1, M):
                    w = splits_at(p, i, m)
                    if w:
                        weight_high(*w)
                    if m in ACT_TILES:
                        evacuate(p, i, n, q, m)
                    if last(n):
                        for what in first_ln.get(m, []):
                            what(0, 0)
                    else:
                        for what, r in extras.get(m, []):
                            what(n + 1, r, (q + 1) % 2) if what is high else what(n + 1, r)

            for r in range(4):
                square(0, r)
            high(0, 0, 0)
            high(0, 1, 0)
            weight_high(0, 0)
            high(0, 2, 0)
            high(0, 3, 0)
            weight_high(0, 1)
            weight_high(0, 2)
            run_blocks(act, proj_block)

            def row_square(R, s, rows):
                act.wait_ge(h_done, R + 1)
                act.activation(out_pair(s)[0:rows, :], hrow[0:rows, s, :], ACT.Square, scale=RMS_SCALE,
                               accum_out=ssq[0:rows, s:s + 1]).then_inc(h_sumsq, 1)

            def step(L, s):
                for r, tile in enumerate(row_tiles(L)):
                    if r == 0 and more(L, 1):
                        squares(L + 1, 1 - s)
                    row_square(*tile)
                    if more(L, 1) and r < 3:
                        (mixed_a_high, silus, mixed_b_high)[r](L + 1, 1 - s)

            run_steps(act, step)

        @block.vector
        def _(dve):
            def low(N, r, q):
                dve.wait_ge(x_hi, 4 * N + r + 1)
                cols = slice(P * r, P * r + ROWS[r])
                dve.tensor_tensor(xT[q][:, 1, :, cols], turned(N, r)[:, :, 0:ROWS[r]],
                                  xT[q][:, 0, :, cols].bitcast(F32), ALU.subtract).then_inc(x_lo, 1)

            def weight_low(p, m):
                c = M * p + m
                dve.wait_ge(w_hi, c + 1)
                hi, lo = slot(m)
                dve.tensor_tensor(lo, raw[:, c % 2, :], hi.bitcast(F32), ALU.subtract).then_inc(w_lo, 1)

            def window_edges(p, i, n):
                need(dve, taps_done, NT * n)
                if first(i):
                    js = slice(2 * p, 2 * p + 2)
                    need(dve, state_out, 64 * p)
                    dve.tensor_copy(v[:, :, 0:HB], hist_b[:, js, :]).then_inc(edges, 1)
                    dve.memset(v[:, :, HB + SAMPLE:2 * HB + SAMPLE], 0.0).then_inc(edges, 1)
                    dve.tensor_copy(u[:, :, UH0:UH0 + HA], hist_a[:, js, :]).then_inc(edges, 1)
                    dve.memset(u[:, :, UH0 + HA + SAMPLE:P0 + HA], 0.0).then_inc(edges, 1)
                    dve.memset(u[:, :, 0:UH0], 0.0).then_inc(edges, 1)
                else:
                    dve.wait_ge(state_out, 64 * p + 32)
                    dve.tensor_copy(v[:, :, VH:VH + HB], v[:, :, VW - HB:VW]).then_inc(edges, 1)
                    dve.tensor_copy(u[:, :, 0:HA], u[:, :, UW - HA:UW]).then_inc(edges, 1)

            def make_v(p, i, n, q, j):
                if j == 0:
                    dve.wait_ge(edges, edge_count(p, i))
                dve.wait_ge(act_evac, 8 * n + 1 + j)
                dve.wait_ge(projected, M * n + AT["a", j] + 1)
                bank = (2 * q + AT["a", j]) % PROJ_BANKS
                parts = [(HB, S0, SAMPLE), (VH + HB + P0, P0, TB - P0)] if first(i) else [(VH + HB, 0, TB)]
                for at, c, w in parts:
                    dve.tensor_tensor(v[:, j, at:at + w], ps[:, bank, c:c + w], tmp[:, j, c:c + w],
                                      ALU.mult).then_inc(v_ready, 1)

            def tap(p, i, n, x):
                j, k = TAPS[x]
                a, w = (0, ACCW) if first(i) else (AC0, TB)
                window, dst = v[:, j, a + k:a + k + w], acc[:, j, a:a + w]
                jj = 2 * p + j
                if k == 0:
                    if j == 0:
                        need(dve, conv_out, 16 * n)
                        if not first(i) or p:
                            dve.wait_ge(conv_out0, 16 * (p + (not first(i))))
                    dve.wait_ge(v_ready, v_count(p, i, j))
                    dve.tensor_scalar(dst, window, wb[:, jj, 0:1], bias_b[:, jj:jj + 1], ALU.mult,
                                      ALU.add).then_inc(taps_done, 1)
                else:
                    dve.wait_ge(taps_done, NT * n + TAP_AT[j, k - 1] + 1)
                    dve.scalar_tensor_tensor(dst, window, wb[:, jj, k:k + 1], dst, ALU.mult,
                                             ALU.add).then_inc(taps_done, 1)

            def conv_a(p, i, n, q, j):
                dve.wait_ge(act_evac, 8 * n + (5 if j == 0 else 7))
                dve.wait_ge(projected, M * n + AT["c", j] + 1)
                bank = (2 * q + AT["c", j]) % PROJ_BANKS
                parts = [(UH0 + HA, S0, SAMPLE), (HA + P0, P0, TB - P0)] if first(i) else [(HA, 0, TB)]
                need(dve, gated, gated_count(p, i, j, "u", back=len(parts)))
                for at, c, w in parts:
                    dve.tensor_tensor(u[:, j, at:at + w], ps[:, bank, c:c + w], tmp[:, 0, c:c + w],
                                      ALU.mult).then_inc(gated, 1)
                jj = 2 * p + j
                for k in range(KA):
                    dve.wait_ge(gated, gated_count(p, i, j, "taps", back=KA - k))
                    if k == 0:
                        dve.tensor_scalar(ca[:, :], u[:, j, 0:TB], wa[:, jj, 0:1], None,
                                          ALU.mult).then_inc(gated, 1)
                    else:
                        dve.scalar_tensor_tensor(ca[:, :], u[:, j, k:k + TB], wa[:, jj, k:k + 1],
                                                 ca[:, :], ALU.mult, ALU.add).then_inc(gated, 1)

            def halves(i):
                return [(UH0, S0, SAMPLE), (P0, P0, TB - P0)] if first(i) else [(0, 0, TB)]

            def gate_b(p, i, n, q, j):
                dve.wait_ge(projected, M * n + AT["b", j] + 1)
                dve.wait_ge(gated, gated_count(p, i, j, "taps"))
                bank = (2 * q + AT["b", j]) % PROJ_BANKS
                for a, c, w in halves(i):
                    dve.tensor_tensor(ca[:, a:a + w], ps[:, bank, c:c + w], ca[:, a:a + w],
                                      ALU.mult).then_inc(gated, 1)

            def gate_z(p, i, n, q, j):
                dve.wait_ge(act_evac, 8 * n + (6 if j == 0 else 8))
                dve.wait_ge(gated, gated_count(p, i, j, "b"))
                for a, c, w in halves(i):
                    dve.tensor_tensor(tmp[:, 1, c:c + w], ca[:, a:a + w], tmp[:, 1, c:c + w],
                                      ALU.mult).then_inc(gated, 1)

            serve = {AT["a", 0]: (make_v, 0), AT["a", 1]: (make_v, 1), AT["c", 0]: (conv_a, 0),
                     AT["b", 0]: (gate_b, 0), AT["z", 0]: (gate_z, 0), AT["c", 1]: (conv_a, 1),
                     AT["b", 1]: (gate_b, 1), AT["z", 1]: (gate_z, 1)}
            lows = {3: 0, 5: 1, 9: 2, 10: 3}
            tap_stops_last = {1: 8, 3: 14, 4: 20, 5: 26, 6: 34, 7: 38, 8: 42, 10: 50, 11: 54}

            def chained(L, k, instruction):
                need(dve, ln, ln_event(L, k - 1))
                instruction().then_inc(ln, 1)

            def centre(L, s):
                w = ln_width(L)
                dve.wait_ge(ln_mean, L + 1)
                mean = ps[:, 4, 0:w].unsqueeze(1).to_broadcast([P, JT, w])
                chained(L, 1, lambda: dve.tensor_tensor(cb[s][:, :, 0:w], cb[s][:, :, 0:w], mean, ALU.subtract))

            def square_sums(L, s):
                w = ln_width(L)
                dve.wait_ge(ln_sq, 2 * L + 2)
                chained(L, 2, lambda: dve.tensor_tensor(tb[:, :, 0:w], tb[:, :, 0:w], ta[:, :, 0:w], ALU.add))
                chained(L, 3, lambda: dve.tensor_tensor(tb[:, 0, 0:w], tb[:, 0, 0:w], tb[:, 1, 0:w], ALU.add))

            def normalise(L, s):
                w = ln_width(L)
                var, y, t = ps[:, 5, 0:w], ta[:, 0, 0:w], ta[:, 1, 0:w]
                dve.wait_ge(ln_var, L + 1)
                chained(L, 4, lambda: dve.tensor_scalar(y, var, LN_EPS, None, ALU.add))
                chained(L, 5, lambda: dve.tensor_scalar(y.bitcast(I32), y.bitcast(I32), -0.5, RSQRT_SEED,
                                                        ALU.mult, ALU.add))
                for k in range(3):
                    chained(L, 6 + 3 * k, lambda: dve.scalar_tensor_tensor(t, y, -0.5, y, ALU.mult, ALU.mult))
                    chained(L, 7 + 3 * k, lambda: dve.scalar_tensor_tensor(t, var, LN_EPS, t, ALU.add, ALU.mult))
                    chained(L, 8 + 3 * k, lambda: dve.scalar_tensor_tensor(y, t, 1.5, y, ALU.add, ALU.mult))
                yb = y.unsqueeze(1).to_broadcast([P, JT, w])
                chained(L, 15, lambda: dve.tensor_tensor(cb[s][:, :, 0:w], cb[s][:, :, 0:w], yb, ALU.mult))

            def gate(L, s):
                w = ln_width(L)
                dve.wait_ge(zt_in[s], 8 * (L - s) + 16)
                dve.wait_ge(ln_silu, 4 * L + 4)
                chained(L, 16, lambda: dve.tensor_tensor(cb[s][:, :, 0:w], cb[s][:, :, 0:w],
                                                         MIX_F32[s][:, 0, JT:, 0:w], ALU.mult))

            def b_low(L, s):
                w = ln_width(L)
                dve.wait_ge(b_hi, L + 1)
                chained(L, 17, lambda: dve.tensor_tensor(MIX[s][:, 0, JT:, 0:w], cb[s][:, :, 0:w],
                                                         MIX[s][:, 1, JT:, 0:w].bitcast(F32), ALU.subtract))

            first_ln = {LN_AT["centre"]: [centre], LN_AT["square_sums"]: [square_sums],
                        LN_AT["normalise"]: [normalise], LN_AT["gate"]: [gate]}

            def proj_block(p, i, n, q):
                done = 0
                stops = tap_stops_last if last(n) else TAP_STOPS
                window_edges(p, i, n)
                for m in range(M):
                    w = splits_at(p, i, m)
                    if w and w[0] < PASSES:
                        weight_low(*w)
                    if last(n):
                        for what in first_ln.get(m, []):
                            what(0, 0)
                    if m in serve:
                        serve[m][0](p, i, n, q, serve[m][1])
                    for x in range(done, stops.get(m, done)):
                        tap(p, i, n, x)
                    done = max(done, stops.get(m, done))
                    if m in lows and not last(n):
                        low(n + 1, lows[m], (q + 1) % 2)
                if last(n):
                    b_low(0, 0)
                for x in range(done, NT):
                    tap(p, i, n, x)

            def scale_first(r):
                rows = rows_at(0, r)[0:ROWS[r], :]
                dve.wait_ge(x_rstd, r + 1)
                dve.tensor_scalar(rows, rows, rstd[0:ROWS[r], r:r + 1], None, ALU.mult).then_inc(x_scaled, 1)

            for r in range(4):
                scale_first(r)
            low(0, 0, 0)
            low(0, 1, 0)
            weight_low(0, 0)
            low(0, 2, 0)
            low(0, 3, 0)
            weight_low(0, 1)
            weight_low(0, 2)
            dve.wait_ge(const_in, 112)
            run_blocks(dve, proj_block)

            def add_residual(R, s, rows):
                dve.wait_ge(out_done, R + 1)
                dve.wait_ge(res_in[s], 8 * (R - s) + 16)
                need(dve, y_out[s], 8 * (R - s))
                dve.tensor_tensor(hrow[0:rows, s, :], out_pair(s)[0:rows, :], raw[0:rows, s, :],
                                  ALU.add).then_inc(h_done, 1)

            def finish_rows(R, s, rows):
                dve.wait_ge(h_rstd, R + 1)
                dve.scalar_tensor_tensor(hrow[0:rows, s, :], hrow[0:rows, s, :], rstd[0:rows, s:s + 1],
                                         fgain[0:rows, :], ALU.mult, ALU.mult).then_inc(y_done, 1)

            def step(L, s):
                tiles = row_tiles(L)
                n1, o = not is_last(L), 1 - s
                if n1:
                    centre(L + 1, o)
                    square_sums(L + 1, o)
                add_residual(*tiles[0])
                if n1:
                    normalise(L + 1, o)
                finish_rows(*tiles[0])
                if len(tiles) > 1:
                    add_residual(*tiles[1])
                if n1:
                    gate(L + 1, o)
                if len(tiles) > 1:
                    finish_rows(*tiles[1])
                if len(tiles) > 1:
                    add_residual(*tiles[2])
                if n1:
                    b_low(L + 1, o)
                if len(tiles) > 1:
                    finish_rows(*tiles[2])
                if len(tiles) > 1:
                    add_residual(*tiles[3])
                    finish_rows(*tiles[3])

            dve.wait_ge(fg_in, 16)
            run_steps(dve, step)

        @block.tensor
        def _(pe):
            def split_product(out, terms):
                mm = None
                for x, (ahi, alo, bhi, blo) in enumerate(terms):
                    pe.matmul(out, ahi, bhi, start=(x == 0), stop=False)
                    pe.matmul(out, ahi, blo, start=False, stop=False)
                    mm = pe.matmul(out, alo, bhi, start=False, stop=(x == len(terms) - 1))
                return mm

            def transposes(N, r):
                rows = ROWS[r]
                pe.wait_ge(x_scaled, 4 * N + r + 1)
                for k in range(KC):
                    mm = pe.transpose(turned(N, r)[:, k, 0:rows], rows_at(N, r)[0:rows, P * k:P * (k + 1)],
                                      ident[0:rows, 0:rows])
                mm.then_inc(x_turned, 1)

            def project(p, i, n, q, m):
                if m == 0:
                    pe.wait_ge(x_lo, 4 * n + 4)
                if first(i):
                    pe.wait_ge(w_lo, M * p + m + 1)
                b = (m - PROJ_BANKS) % M
                kind, j = TILES[b]
                if m < PROJ_BANKS:
                    if b in ACT_TILES:
                        need(pe, act_evac, 8 * (n - 1) + ACT_TILES.index(b) + 1)
                    else:
                        need(pe, gated, gated_count_before(p, i, "u" if kind == "c" else "b"))
                elif b in ACT_TILES:
                    pe.wait_ge(act_evac, 8 * n + ACT_TILES.index(b) + 1)
                elif kind == "a":
                    pe.wait_ge(v_ready, v_count(p, i, j))
                else:
                    pe.wait_ge(gated, gated_count(p, i, j, "u" if kind == "c" else "b"))
                hi, lo = slot(m)
                x = xT[q]
                split_product(ps[:, (2 * q + m) % PROJ_BANKS, 0:TB],
                              [(hi[:, P * k:P * (k + 1)], lo[:, P * k:P * (k + 1)], x[:, 0, k, :], x[:, 1, k, :])
                               for k in range(KC)]).then_inc(projected, 1)

            def channel_mean(L, dst, src, done):
                w = ln_width(L)
                pe.matmul(dst[:, 0:w], mean_w[:, :], src[:, 0:w], start=True, stop=True).then_inc(done, 1)

            def mean(L):
                pe.wait_ge(ln_sum, 2 * L + 2)
                channel_mean(L, ps[:, 4, :], ta[:, 0, :], ln_mean)

            def var(L):
                pe.wait_ge(ln, ln_event(L, 3))
                channel_mean(L, ps[:, 5, :], tb[:, 0, :], ln_var)

            def proj_block(p, i, n, q):
                for m in range(M):
                    if m in TRANSPOSE_AT and not last(n):
                        transposes(n + 1, TRANSPOSE_AT[m])
                    if last(n) and m == LN_AT["centre"]:
                        mean(0)
                    if last(n) and m == LN_AT["normalise"]:
                        var(0)
                    project(p, i, n, q, m)

            pe.wait_ge(ready0, 5)
            for r in range(4):
                transposes(0, r)
            run_blocks(pe, proj_block)

            def rows_out(L, s, r, R, rs):
                pe.wait_ge(a_lo, L + 1)
                pe.wait_ge(ln, ln_event(L, LN_OPS))
                need(pe, h_sumsq, R - 1)
                mx = MIX[s]
                for half_d in range(2):
                    cols = slice(512 * half_d, 512 * half_d + 512)
                    terms = []
                    for e in range(KC):
                        hi, lo = slot(e)
                        terms.append((mx[:, 1, e, P * r:P * (r + 1)], mx[:, 0, e, P * r:P * (r + 1)],
                                      hi[:, cols], lo[:, cols]))
                    mm = split_product(ps[:, 2 * rs + half_d, :], terms)
                mm.then_inc(out_done, 1)

            def step(L, s):
                n1 = not is_last(L)
                if n1:
                    mean(L + 1)
                for r, (R, rs, _) in enumerate(row_tiles(L)):
                    rows_out(L, s, r, R, rs)
                    if n1 and r == 0:
                        var(L + 1)

            pe.wait_ge(act_evac, 8 * (LAST + 1))
            pe.wait_ge(gated, gated_count(1, BLOCKS - 1, 1, "b"))
            pe.wait_ge(w_lo, M * PASSES + KC)
            run_steps(pe, step)


def kernel(**inputs):
    import numpy as _np
    import concourse.bacc as _bacc
    from concourse import mybir as _mybir
    from concourse.bass_utils import run_bass_kernel_spmd as _run

    c = _np.ascontiguousarray
    g = {k: _np.asarray(a) for k, a in inputs.items()}
    n_tiles = g["w_in"].shape[2] // P
    by_tile = lambda a: c(a.reshape(-1, P).T)
    arrays = {
        "x_prompt": c(g["x_prompt"][0]),
        "x_sample": c(g["x_sample"][0]),
        "state_conv_a": c(g["state_conv_a"][0, 0].T),
        "state_conv_b": c(g["state_conv_b"][0, 0].T),
        "norm_g": by_tile(g["norm_g"][0]),
        "w_in": c(g["w_in"][0].reshape(KC, P, n_tiles, P).transpose(2, 1, 0, 3)).reshape(n_tiles, P, D),
        "conv_a_w": c(g["conv_a_w"][0].T),
        "conv_b_w": c(g["conv_b_w"][0].T),
        "conv_b_bias": by_tile(g["conv_b_bias"][0]),
        "ln_b_g": by_tile(g["ln_b_g"][0]),
        "ln_b_b": by_tile(g["ln_b_b"][0]),
        "w_out": c(g["w_out"][0]),
        "final_norm_g": c(g["final_norm_g"][None, :]),
    }
    outs = {
        "y_prompt": (SEQ, D), "y_sample": (SAMPLE, D),
        "new_a_prompt": (DA, HA), "new_b_prompt": (DA, HB),
        "new_a_sample": (DA, HA), "new_b_sample": (DA, HB),
    }
    nc = _bacc.Bacc("TRN2", target_bir_lowering=False, num_devices=1)
    A, feed = {}, {}
    for name, a in arrays.items():
        feed[f"in_{name}"] = a
        A[name] = nc.dram_tensor(f"in_{name}", a.shape, _mybir.dt.from_np(a.dtype), kind="ExternalInput").ap()
    for name, shape in outs.items():
        A[name] = nc.dram_tensor(f"out_{name}", shape, F32, kind="ExternalOutput").ap()
    build_program(nc, A)
    r = _run(nc, [feed], core_ids=[0]).results[0]
    state = lambda name: c(r[f"out_{name}"].T)[None, None]
    return (r["out_y_prompt"][None], r["out_y_sample"][None], state("new_a_prompt"), state("new_b_prompt"),
            state("new_a_sample"), state("new_b_sample"))
```

```python
import concourse.bass as bass
from concourse import mybir
from contextlib import ExitStack

F32 = mybir.dt.float32
F32R = mybir.dt.float32r
I32 = mybir.dt.int32
ALU = mybir.AluOpType
ACT = mybir.ActivationFunctionType

P = 128
D = 1024
KC = D // P
DA = 512
JT = DA // P
SEQ, SAMPLE = 4096, 32
KA, KB = 3, 31
HA, HB = KA - 1, KB - 1
RMS_EPS, LN_EPS = 1e-6, 1e-5
RMS_SCALE = D ** -0.5

PASSES = 2
BLOCKS = 9
TB = 460
PAD = BLOCKS * TB - SEQ - SAMPLE
S0, P0 = PAD, PAD + SAMPLE
TOK = BLOCKS * TB
STAT_COLS = 4
STAT_ROWS = TB // STAT_COLS

VW = HB + SAMPLE + HB + (TB - P0)
VH = VW - TB - HB
UW = HA + TB
UH0 = UW - (HA + SAMPLE + HA + TB - P0)
ACCW = VW - HB
AC0 = ACCW - TB

TILES = [("g", 0), ("a", 0), ("g", 1), ("a", 1), ("zb", 0), ("zb", 1), ("h", 0), ("c", 0),
         ("b", 0), ("z", 0), ("h", 1), ("c", 1), ("b", 1), ("z", 1)]
SECTION = {"h": 0, "b": 1, "c": 2, "z": 3, "a": 4, "g": 5, "zb": 6}
M = len(TILES)
AT = {t: m for m, t in enumerate(TILES)}
ACT_TILES = [m for m, (k, _) in enumerate(TILES) if k in ("g", "zb", "h", "z")]
PROJ_BANKS = 7
STAT_BANK = 7
SLOT = 2 * D
LEAD = 3
EARLY = 8


def splits_at(p, i, m):
    if not isinstance(i, int):
        return None
    if p == 0 and i == 0:
        return (0, m + LEAD) if 0 <= m and m + LEAD < M else None
    if i == 0:
        return (p, EARLY + m) if 0 <= m and EARLY + m < M else None
    if i == BLOCKS - 1:
        return (p + 1, m - 2) if 2 <= m < 2 + EARLY else None
    return None


LN_AT = {"centre": 3, "square_sums": 5, "var_low": 6, "normalise": 7, "gate": 11, "b_low": 13}
TAPS = [(0, k) for k in range(13)]
_a, _b = [(1, k) for k in range(KB)], [(0, k) for k in range(13, KB)]
for _k in range(KB):
    TAPS.append(_a[_k])
    if _k < len(_b):
        TAPS.append(_b[_k])
NT = len(TAPS)
TAP_AT = {t: x for x, t in enumerate(TAPS)}
TAP_STOPS = {1: 13, 3: 22, 4: 29, 5: 36, 6: 43, 7: 45, 8: 48, 9: 50, 10: 54, 11: 57, 12: NT}
SQUARE_AT = {0: 0, 1: 1}
RSTD_AT = 7
SCALE_AT = [{8: 0, 9: 1}, {2: 0, 3: 1}]
HIGH_AT = [{10: 0, 11: 1}, {4: 0, 5: 1}]
LOW_AT = [{11: 0, 12: 1}, {5: 0, 6: 1}]
HALF = KC // 2

OB = 512
RT = OB // P
OBLOCKS = SEQ // OB
LN_OPS = 18
SAMPLE_ROWS = SEQ // P
RSQRT_SEED = 1597463007.0


def build_program(nc, A):
    ctx = ExitStack()
    with ctx:
        def sb(name, shape, dt=F32, scope=ctx):
            return scope.enter_context(nc.sbuf_tensor(name, shape, dt))

        def sb_two(name, shape, scope=ctx):
            with ExitStack() as short:
                split = sb(name, shape, F32R, short)
            return split, sb(f"{name}_f32", shape, F32, scope)

        def sem(name):
            return ctx.enter_context(nc.semaphore(name))

        conv_d = nc.dram_tensor("conv_spill", [DA, TOK], F32).ap()
        zb_d = nc.dram_tensor("zb_spill", [DA, TOK], F32).ap()
        outa_d = nc.dram_tensor("outa_spill", [DA, TOK], F32).ap()
        rstd_d = nc.dram_tensor("rstd_spill", [1, BLOCKS * P * STAT_COLS], F32).ap()

        W, W_f32 = sb_two("w_split", [P, 12 * SLOT])
        raw = sb("w_raw", [P, 2, D])
        ident = sb("ident", [P, P])
        mean_w, mean_w_f32 = sb_two("mean_w", [P, P])
        gain = sb("gain", [P, KC])
        wb = sb("conv_b_taps", [P, JT, KB])
        bias_b = sb("conv_b_bias_sb", [P, JT])
        wa = sb("conv_a_taps", [P, JT, KA])
        hist_b = sb("hist_b", [P, JT, HB])
        hist_a = sb("hist_a", [P, JT, HA])
        ln_g = sb("ln_g", [P, JT])
        ln_b = sb("ln_b", [P, JT])
        minus_half = sb("minus_half", [P, 1])
        eps = sb("rms_eps", [P, 1])
        ones = sb("ones", [P, 1])
        x_var = sb("x_mean_square_eps", [P, STAT_COLS])
        x_rs = sb("x_rstd_columns", [P, STAT_COLS])
        ssq = sb("row_mean_sq", [P, 2])
        mean_sq = sb("row_mean_sq_eps", [P, 2])
        rstd = sb("rstd", [P, 2])
        early = ExitStack()
        xT0, xT0_f32 = sb_two("xT0", [P, 2, KC, TB], early)
        spread = sb("rstd_spread", [P, TB], F32, early)
        sb("early_gap", [P, 4 * OB - TB], F32, early)
        W2 = sb("w_split_2", [P, 2 * SLOT], F32R, early)
        xT1, xT1_f32 = sb_two("xT1", [P, 2, KC, TB], early)
        xT, xT_f32 = [xT0, xT1], [xT0_f32, xT1_f32]
        v = sb("v", [P, 2, VW], F32, early)
        u = sb("u", [P, 2, UW], F32, early)
        tmp = sb("gates", [P, 2, TB], F32, early)
        acc = sb("conv_b_acc", [P, 2, ACCW], F32, early)
        szb = sb("szb", [P, TB], F32, early)
        ca = sb("conv_a_acc", [P, TB], F32, early)
        early.close()
        cb = [sb(f"conv_b_{s}", [P, JT, OB]) for s in range(2)]
        fgain = sb("final_gain", [P, D])
        hrow = sb("h_rows", [P, 2, D])
        sb("gap", [P, 2 * KC * TB - 2 * JT * OB - 3 * D])
        ta_split, ta = sb_two("ln_tmp_a", [P, 2, OB])
        tb_split, tb = sb_two("ln_tmp_b", [P, 2, OB])
        mix2, mix2_f32 = sb_two("mixed_1", [P, 2, 2 * JT, OB])

        def slot(m):
            t, n = (W, m) if m < 12 else (W2, m - 12)
            return t[:, n * SLOT:n * SLOT + D], t[:, n * SLOT + D:(n + 1) * SLOT]

        mix1, mix1_f32 = (t[:, 8 * SLOT:12 * SLOT].rearrange("p (l e t) -> p l e t", l=2, t=OB)
                          for t in (W, W_f32))
        MIX = [mix1, mix2[:, :, :, :]]
        MIX_F32 = [mix1_f32, mix2_f32[:, :, :, :]]

        ps = ctx.enter_context(nc.psum_tensor("ps", [P, 8, 512], F32))

        def x_stats(N):
            if isinstance(N, int) and N == 0:
                return ps[0:STAT_ROWS, 0:STAT_COLS, 0]
            return ps[0:STAT_ROWS, STAT_BANK, 0:STAT_COLS]

        def chunks_of(q, part, a, b):
            return xT_f32[q][:, part, a:b, :]

        def half_of(q, h, part):
            return chunks_of(q, part, HALF * h, HALF * (h + 1))

        QUARTERS = [(2 * r, 2 * r + 2) for r in range(4)]

        def out_pair(s):
            return ps[:, 2 * s:2 * s + 2, :].rearrange("p b t -> p (b t)")

        const_in = sem("const_in")
        ready0 = sem("pool_consts_ready")
        mean_w_ready = sem("mean_weights_ready")
        gain_in = sem("norm_g_in")
        x_in = [sem(f"xT_in_{h}") for h in range(2)]
        x_sq = sem("x_squares")
        x_sum = sem("x_squares_summed")
        x_sum0 = sem("x_squares_summed_first")
        x_stat = sem("x_mean_square")
        x_ms = sem("x_mean_square_eps")
        x_rstd = sem("x_rstd")
        x_rstd_out = sem("x_rstd_out")
        x_spread = sem("x_rstd_spread")
        x_spread0 = sem("x_rstd_spread_first")
        x_scaled0 = sem("x_scaled_first")
        x_scaled = sem("x_scaled")
        x_hi = sem("x_hi")
        x_lo = sem("x_lo")
        w_in_s = [sem(f"w_raw_in_{s}") for s in range(2)]
        w_scaled = sem("w_scaled")
        w_scaled_a = sem("w_scaled_by_scalar")
        w_hi = sem("w_hi")
        w_lo_v = sem("w_lo_by_vector")
        w_lo_p = sem("w_lo_by_pool")
        projected = sem("projected")
        act_evac = sem("act_evacuated")
        edges = sem("window_edges")
        v_ready = sem("v_ready")
        taps_done = sem("taps_done")
        gated = sem("gated_steps")
        conv_out = sem("conv_out")
        conv_out0 = sem("conv_out_sample")
        zb_out = sem("zb_out")
        outa_out = sem("outa_out")
        state_out = sem("state_out")
        fg_in = sem("final_gain_in")
        cb_in = [sem(f"conv_b_in_{s}") for s in range(2)]
        zt_in = [sem(f"silu_zb_in_{s}") for s in range(2)]
        oa_in = [sem(f"out_a_in_{s}") for s in range(2)]
        ln_sum = sem("ln_sums")
        ln_sum_hi = sem("ln_sum_hi")
        ln_sum_lo = sem("ln_sum_lo")
        ln_var_hi = sem("ln_square_sum_hi")
        ln = sem("ln_steps")
        ln_mean = sem("ln_mean")
        ln_sq = sem("ln_squares")
        ln_var = sem("ln_var")
        ln_silu = sem("ln_silu")
        a_hi = sem("mixed_a_hi")
        a_lo = sem("mixed_a_lo")
        b_hi = sem("mixed_b_hi")
        out_done = sem("rows_multiplied")
        res_in = [sem(f"residual_in_{s}") for s in range(2)]
        h_done = sem("h_done")
        h_sumsq = sem("h_sumsq")
        h_ms = sem("h_mean_square")
        h_rstd = sem("h_rstd")
        y_done = sem("y_done")
        y_out = [sem(f"y_out_{s}") for s in range(2)]

        def by_vector(c):
            return c < M * PASSES and c % 2 == 0

        def by_scalar(c):
            return LEAD <= c < M * PASSES and c % 2 == 0

        SCALED_BY_SCALAR = [c for c in range(M * PASSES) if by_scalar(c)]

        def weight_split(c):
            if by_vector(c):
                return w_lo_v, c // 2 + 1
            in_passes = M * PASSES
            return w_lo_p, c // 2 + 1 if c < in_passes else in_passes // 2 + c - in_passes + 1

        def need(eng, s, value):
            if not (isinstance(value, int) and value <= 0):
                eng.wait_ge(s, value)

        def v_count(p, i, j):
            return 20 * p + 2 * (j + 1) if first(i) else 20 * p + 3 + 2 * i + j

        STEP = {"u": (2, 1), "taps": (5, 4), "b": (7, 5), "out": (9, 6)}

        def gated_count(p, i, j, what, back=0):
            if first(i):
                return 114 * p + 9 * j + STEP[what][0] - back
            return 114 * p + 6 + 12 * i + 6 * j + STEP[what][1] - back

        def gated_count_before(p, i, j, what):
            if first(i):
                return gated_count(p - 1, BLOCKS - 1, j, what) if p else 0
            return 114 * p + 12 * i - 6 + 6 * j + STEP[what][1]

        def edge_count(p, i):
            return 21 * p + 5 if first(i) else 21 * p + 5 + 2 * i

        def first(i):
            return isinstance(i, int) and i == 0

        def run_blocks(eng, block, peeled=1):
            for p in range(PASSES):
                pairs = (BLOCKS - peeled) // 2 - 1
                for i in range(peeled):
                    block(p, i, i + BLOCKS * p, (BLOCKS * p + i) % 2)
                with eng.Fori(0, pairs) as it:
                    for o in range(2):
                        i = 2 * it + (peeled + o)
                        block(p, i, i + BLOCKS * p, (BLOCKS * p + peeled + o) % 2)
                for i in range(peeled + 2 * pairs, BLOCKS):
                    block(p, i, i + BLOCKS * p, (BLOCKS * p + i) % 2)

        def following(p, i):
            return (p + 1, 0) if isinstance(i, int) and i == BLOCKS - 1 else (p, i + 1)

        LAST = PASSES * BLOCKS - 1

        def last(n):
            return isinstance(n, int) and n == LAST

        def ln_cols(L):
            return S0 if is_last(L) else P0 + L * OB

        def ln_width(L):
            return P if is_last(L) else OB

        def run_steps(eng, step):
            for L in (0, 1):
                step(L, L % 2)
            with eng.Fori(0, (OBLOCKS - 4) // 2) as it:
                for o in range(2):
                    step(2 * it + (2 + o), o)
            for L in range(OBLOCKS - 2, OBLOCKS + 1):
                step(L, L % 2)

        def row_tiles(L):
            if is_last(L):
                return [(SAMPLE_ROWS, 0, SAMPLE)]
            return [(RT * L + r, r % 2, P) for r in range(RT)]

        def more(L, ahead):
            return not (isinstance(L, int) and L + ahead > OBLOCKS)

        def is_last(L):
            return isinstance(L, int) and L == OBLOCKS

        def ln_event(L, k):
            return LN_OPS * L + k

        block = ctx.enter_context(nc.Block())

        @block.sync
        def _(sp):
            chan = lambda t: t.rearrange("(j p) k -> p j k", p=P)
            consts = [(wb[:, :, :], chan(A["conv_b_w"])), (wa[:, :, :], chan(A["conv_a_w"])),
                      (hist_b[:, :, :], chan(A["state_conv_b"])), (hist_a[:, :, :], chan(A["state_conv_a"])),
                      (bias_b[:, :], A["conv_b_bias"]),
                      (ln_g[:, :], A["ln_b_g"]), (ln_b[:, :], A["ln_b_b"])]

            def load_x(i, q, h):
                src = A["xT"][i, :, h]
                sp.dma_start(half_of(q, h, 1), src.rearrange("p (k t) -> p k t", t=TB)).then_inc(x_in[h], 16)

            def send_rstd(i, N):
                sp.wait_ge(x_rstd, N + 1)
                dst = rstd_d[0, bass.ds(P * STAT_COLS * i, TB)].rearrange("(r c) -> r c", c=STAT_COLS)
                sp.dma_start(dst, x_rs[0:STAT_ROWS, :]).then_inc(x_rstd_out, 16)

            def spread_rstd(p, i, N):
                columns = bass.ds(P * STAT_COLS * i, TB)
                if p == 0:
                    sp.wait_ge(x_rstd_out, 16 * (N + 1))
                else:
                    sp.wait_ge(x_scaled, 2 * N)
                sp.dma_start(spread[:, :], rstd_d[:, columns].to_broadcast([P, TB])
                             ).then_inc(x_spread, 16)

            def load_w(p, m):
                c = M * p + m
                if c >= 2:
                    sp.wait_ge(*weight_split(c - 2))
                if p < PASSES:
                    k, j = TILES[m]
                    src = A["w_in"][SECTION[k] * JT + 2 * p + j]
                else:
                    src = A["w_out"][P * m:P * (m + 1), :]
                sp.dma_start(raw[:, c % 2, :], src).then_inc(w_in_s[c % 2], 16)

            def spill(dram, p, j, nj=1):
                return dram[P * (2 * p + j):P * (2 * p + j + nj), :].rearrange("(j p) t -> p j t", p=P)

            def store_conv(p, i, n):
                sp.wait_ge(taps_done, NT * n + NT)
                dst = spill(conv_d, p, 0, 2)
                if first(i):
                    sp.dma_start(dst[:, :, S0:P0], acc[:, :, 0:SAMPLE]).then_inc(conv_out0, 16)
                    sp.dma_start(dst[:, :, P0:TB], acc[:, :, AC0 + P0:]).then_inc(conv_out, 16)
                else:
                    sp.dma_start(dst[:, :, bass.ds(TB * i, TB)], acc[:, :, AC0:]).then_inc(conv_out, 16)

            def store_zb(p, i, n, j):
                sp.wait_ge(act_evac, 8 * n + 3 + j)
                sp.dma_start(spill(zb_d, p, j)[:, 0, bass.ds(TB * i, TB)], szb[:, :]).then_inc(zb_out, 16)

            def store_outa(p, i, n, j):
                sp.wait_ge(gated, gated_count(p, i, j, "out"))
                sp.dma_start(spill(outa_d, p, j)[:, 0, bass.ds(TB * i, TB)], tmp[:, 1, :]).then_inc(outa_out, 16)

            def store_states(p, i, kind):
                vs, us = (HB + SAMPLE - HB, UH0 + SAMPLE) if kind == "sample" else (VW - HB, UW - HA)
                sp.wait_ge(v_ready, v_count(p, i, 1))
                sp.dma_start(spill(A[f"new_b_{kind}"], p, 0, 2), v[:, :, vs:vs + HB]).then_inc(state_out, 16)
                sp.wait_ge(gated, gated_count(p, i, 1, "u"))
                sp.dma_start(spill(A[f"new_a_{kind}"], p, 0, 2), u[:, :, us:us + HA]).then_inc(state_out, 16)

            def load_cb(L, s):
                if not isinstance(L, int) or L >= 2:
                    sp.wait_ge(ln, ln_event(L - 2, LN_OPS))
                w = ln_width(L)
                src = conv_d.rearrange("(j p) t -> p j t", p=P)[:, :, bass.ds(ln_cols(L), w)]
                sp.dma_start(cb[s][:, :, 0:w], src).then_inc(cb_in[s], 16)

            def load_mix(L, s):
                if not isinstance(L, int) or L >= 2:
                    sp.wait_ge(out_done, RT * (L - 1))
                w = ln_width(L)
                for at, dram, arrived in ((0, outa_d, oa_in), (JT, zb_d, zt_in)):
                    if isinstance(L, int) and L == 0:
                        sp.wait_ge(projected, M * LAST + (9 if at == 0 else 10))
                    src = dram.rearrange("(j p) t -> p j t", p=P)[:, :, bass.ds(ln_cols(L), w)]
                    sp.dma_start(MIX_F32[s][:, 0, at:at + JT, 0:w], src).then_inc(arrived[s], 16)

            def proj_block(p, i, n, q):
                nxt = following(p, i)
                for m in range(-1, M):
                    w = splits_at(p, i, m + 1)
                    if w:
                        load_w(*w)
                    if m == -1 and not last(n):
                        need(sp, projected, M * n)
                        for h in range(2):
                            load_x(nxt[1], 1 - q, h)
                    if m == RSTD_AT and nxt[0] == 0:
                        send_rstd(nxt[1], n + 1)
                    if m == (-1 if nxt[0] else RSTD_AT + 1) and not last(n):
                        spread_rstd(*nxt, n + 1)
                    if m == 1 and not first(i):
                        store_conv(p, i - 1, n - 1)
                    if m == -1 and last(n):
                        sp.wait_ge(projected, M * LAST)
                        sp.wait_ge(conv_out, 16 * (LAST - 1))
                        sp.wait_ge(conv_out0, 16 * PASSES)
                        load_cb(0, 0)
                    if m == 3 and last(n):
                        load_cb(1, 1)
                        sp.dma_start(fgain[:, :], A["final_norm_g"].to_broadcast([P, D])).then_inc(fg_in, 16)
                    if m == AT["z", 0] and last(n):
                        sp.wait_ge(zb_out, 32 * (LAST + 1))
                        sp.wait_ge(outa_out, 32 * LAST)
                        load_mix(0, 0)
                    if m in (AT["zb", 0], AT["zb", 1]):
                        store_zb(p, i, n, m - AT["zb", 0])
                    if m in (AT["z", 0], AT["z", 1]):
                        store_outa(p, i, n, int(m == AT["z", 1]))
                if first(i):
                    store_states(p, i, "sample")
                if isinstance(i, int) and i == BLOCKS - 1:
                    store_states(p, i, "prompt")
                    if not last(n):
                        store_conv(p, i, n)

            load_x(0, 0, 0)
            load_x(0, 0, 1)
            sp.dma_start(gain[:, :], A["norm_g"]).then_inc(gain_in, 16)
            load_w(0, 0)
            load_w(0, 1)
            for dst, src in consts:
                sp.dma_start(dst, src).then_inc(const_in, 16)
            send_rstd(0, 0)
            load_w(0, 2)
            run_blocks(sp, proj_block, peeled=3)

            def rows_of(R, name):
                if isinstance(R, int) and R == SAMPLE_ROWS:
                    return A[f"{name}_sample"]
                return A[f"{name}_prompt"][bass.ds(P * R, P), :]

            def load_residual(R, s, rows):
                need(sp, h_done, R - 1)
                src = rows_of(R, "x")
                sp.dma_start(raw[0:rows, s, :], src).then_inc(res_in[s], 16)

            def store_y(R, s, rows):
                sp.wait_ge(y_done, R + 1)
                sp.dma_start(rows_of(R, "y"), hrow[0:rows, s, :]).then_inc(y_out[s], 16)

            def step(L, s):
                if isinstance(L, int) and L == 1:
                    store_conv(PASSES - 1, BLOCKS - 1, LAST)
                    sp.wait_ge(conv_out, 16 * (LAST + 1))
                if more(L, 2):
                    load_cb(L + 2, s)
                for r, (R, rs, rows) in enumerate(row_tiles(L)):
                    if not is_last(L):
                        sample = isinstance(R, int) and R + 1 == SAMPLE_ROWS
                        load_residual(R + 1, (rs + 1) % 2, SAMPLE if sample else P)
                    if r == RT - 1 and more(L, 2):
                        load_mix(L + 2, s)
                    store_y(R, rs, rows)

            sp.wait_ge(*weight_split(M * PASSES + KC - 1))
            load_residual(0, 0, P)
            sp.wait_ge(projected, M * (LAST + 1))
            sp.wait_ge(outa_out, 32 * (LAST + 1))
            load_mix(1, 1)
            sp.wait_ge(conv_out, 16 * LAST)
            sp.wait_ge(state_out, 64 * PASSES)
            run_steps(sp, step)
            sp.wait_ge(y_out[0], 16 * (SEQ // P // 2 + 1))
            sp.wait_ge(y_out[1], 16 * (SEQ // P // 2))

        @block.gpsimd
        def _(pool):
            pool.memset(ones[:, :], 1.0).then_inc(ready0, 1)
            pool.memset(eps[:, :], RMS_EPS).then_inc(ready0, 1)
            pool.memset(minus_half[:, :], -0.5).then_inc(ready0, 1)
            pool.memset(mean_w_f32[:, :], 1.0 / DA).then_inc(ready0, 1)
            pool.memset(ident[:, :], 0.0).then_inc(ready0, 1)
            pool.wait_ge(ready0, 5)
            pool.affine_select(out=ident[:, :], in_=ident[:, :], compare_op=ALU.not_equal, fill=1.0,
                               base=0, pattern=[[-1, P]], channel_multiplier=1).then_inc(ready0, 1)

            def row_rstd(r, rows, count):
                pool.wait_ge(h_sumsq, count)
                pool.tensor_tensor(mean_sq[0:rows, r:r + 1], ssq[0:rows, r:r + 1], eps[0:rows, :],
                                   ALU.add).then_inc(h_ms, 1)
                pool.wait_ge(h_ms, count)
                pool.tensor_tensor(rstd[0:rows, r:r + 1], mean_sq[0:rows, r:r + 1],
                                   minus_half[0:rows, :], ALU.pow).then_inc(h_rstd, 1)

            def x_sum_step(N, q, step):
                if step:
                    pool.wait_ge(x_sum, 4 * (N - 1) + step)
                else:
                    pool.wait_ge(x_sq, 2 * N + 2)
                to, of, k = [(0, 4, 2), (2, 6, 2), (0, 2, 2), (0, 1, 1)][step]
                sq = xT_f32[q][:, 0]
                pool.tensor_tensor(sq[:, to:to + k], sq[:, to:to + k], sq[:, of:of + k], ALU.add).then_inc(x_sum, 1)

            def x_row_rstd(N):
                pool.wait_ge(x_ms, N + 1)
                need(pool, x_rstd_out, 16 * N)
                pool.tensor_tensor(x_rs[0:STAT_ROWS, :], x_var[0:STAT_ROWS, :],
                                   minus_half[0:STAT_ROWS, :].to_broadcast([STAT_ROWS, STAT_COLS]),
                                   ALU.pow).then_inc(x_rstd, 1)

            def x_scale(N, q, a, b):
                pool.wait_ge(x_in[a // HALF], 16 * (N + 1))
                if isinstance(N, int) and N == 0:
                    pool.wait_ge(x_spread0, 2)
                else:
                    pool.wait_ge(x_spread, 16 * N)
                raw_x = chunks_of(q, 1, a, b)
                pool.tensor_tensor(raw_x, raw_x, spread[:, :].unsqueeze(1).to_broadcast([P, b - a, TB]),
                                   ALU.mult).then_inc(x_scaled, 1)

            def scale_w(p, m):
                c = M * p + m
                pool.wait_ge(w_in_s[c % 2], 16 * (c // 2 + 1))
                w = raw[:, c % 2, :].rearrange("p (k c) -> p k c", k=KC)
                pool.tensor_tensor(w, w, gain[:, :].unsqueeze(2).to_broadcast([P, KC, P]),
                                   ALU.mult).then_inc(w_scaled, 1)

            def weight_low(p, m):
                c = M * p + m
                pool.wait_ge(w_hi, c + 1)
                hi, lo = slot(m)
                pool.tensor_tensor(lo, raw[:, c % 2, :], hi.bitcast(F32), ALU.subtract).then_inc(w_lo_p, 1)

            def sums(L, s):
                w = ln_width(L)
                pool.wait_ge(cb_in[s], 8 * (L - s) + 16)
                if not isinstance(L, int) or L >= 1:
                    pool.wait_ge(ln, ln_event(L - 1, 16))
                pool.tensor_tensor(ta[:, :, 0:w], cb[s][:, 0:2, 0:w], cb[s][:, 2:4, 0:w],
                                   ALU.add).then_inc(ln_sum, 1)
                pool.wait_ge(ln_sum, 2 * L + 1)
                pool.tensor_tensor(ta[:, 0, 0:w], ta[:, 0, 0:w], ta[:, 1, 0:w], ALU.add).then_inc(ln_sum, 1)

            def sum_low(L):
                w = ln_width(L)
                pool.wait_ge(ln_sum_hi, L + 1)
                pool.tensor_tensor(ta_split[:, 0, 0:w], ta[:, 0, 0:w], ta_split[:, 1, 0:w].bitcast(F32),
                                   ALU.subtract).then_inc(ln_sum_lo, 1)

            def a_low(L, s):
                w = ln_width(L)
                pool.wait_ge(a_hi, L + 1)
                pool.tensor_tensor(MIX[s][:, 0, 0:JT, 0:w], MIX_F32[s][:, 0, 0:JT, 0:w],
                                   MIX[s][:, 1, 0:JT, 0:w].bitcast(F32), ALU.subtract).then_inc(a_lo, 1)

            def proj_block(p, i, n, q):
                for m in range(-1, M):
                    w = splits_at(p, i, m)
                    if w and not by_vector(M * w[0] + w[1]):
                        weight_low(*w)
                    w = splits_at(p, i, m + 1)
                    if w and w[0] < PASSES and not by_scalar(M * w[0] + w[1]):
                        scale_w(*w)
                    if not last(n):
                        if 1 <= m <= 4 and following(p, i)[0] == 0:
                            x_sum_step(n + 1, 1 - q, m - 1)
                        if m == RSTD_AT and following(p, i)[0] == 0:
                            x_row_rstd(n + 1)
                        scale_at = SCALE_AT[following(p, i)[0]]
                        if m in scale_at:
                            h = scale_at[m]
                            x_scale(n + 1, 1 - q, HALF * h, HALF * (h + 1))
                    if last(n) and m == 1:
                        sums(0, 0)
                        sum_low(0)
                    if last(n) and m == M - 4:
                        sums(1, 1)
                        sum_low(1)
                    if last(n) and m == M - 2:
                        a_low(0, 0)

            pool.wait_ge(gain_in, 16)
            scale_w(0, 0)
            x_row_rstd(0)
            scale_w(0, 1)
            x_scale(0, 0, *QUARTERS[2])
            x_scale(0, 0, *QUARTERS[3])
            weight_low(0, 1)
            scale_w(0, 2)
            run_blocks(pool, proj_block)

            def step(L, s):
                for r, (R, rs, rows) in enumerate(row_tiles(L)):
                    row_rstd(rs, rows, R + 1)
                    if r == 0 and more(L, 1):
                        a_low(L + 1, 1 - s)
                    if r == 1 and more(L, 2):
                        sums(L + 2, s)
                        sum_low(L + 2)

            run_steps(pool, step)

        @block.scalar
        def _(act):
            def square(N, q, h):
                act.wait_ge(x_in[h], 16 * (N + 1))
                act.activation(half_of(q, h, 0), half_of(q, h, 1), ACT.Square,
                               scale=RMS_SCALE).then_inc(x_sq, 1)

            def x_mean_square(N):
                act.wait_ge(x_stat, N + 1)
                act.activation(x_var[0:STAT_ROWS, :], x_stats(N), ACT.Identity,
                               bias=eps[0:STAT_ROWS, :]).then_inc(x_ms, 1)

            def high(N, q, h):
                act.wait_ge(x_scaled, 2 * N + h + 1)
                act.activation(xT[q][:, 0, HALF * h:HALF * (h + 1), :], half_of(q, h, 1), ACT.Copy).then_inc(x_hi, 1)

            def high_first(r):
                act.wait_ge(*[(x_scaled0, 1), (x_scaled0, 2), (x_scaled, 1), (x_scaled, 2)][r])
                a, b = QUARTERS[r]
                act.activation(xT[0][:, 0, a:b, :], chunks_of(0, 1, a, b), ACT.Copy).then_inc(x_hi, 1)

            def weight_high(p, m):
                c = M * p + m
                if by_scalar(c):
                    act.wait_ge(w_in_s[c % 2], 16 * (c // 2 + 1))
                    for k in range(KC):
                        w = raw[:, c % 2, P * k:P * (k + 1)]
                        act.activation(w, w, ACT.Copy, scale=gain[:, k:k + 1]).then_inc(w_scaled_a, 1)
                    act.wait_ge(w_scaled_a, KC * (SCALED_BY_SCALAR.index(c) + 1))
                elif p < PASSES:
                    act.wait_ge(w_scaled, c + 1 - len([b for b in SCALED_BY_SCALAR if b < c]))
                else:
                    act.wait_ge(w_in_s[c % 2], 16 * (c // 2 + 1))
                if p:
                    act.wait_ge(projected, M * (BLOCKS * p - 1) + m + 1)
                act.activation(slot(m)[0], raw[:, c % 2, :], ACT.Copy).then_inc(w_hi, 1)

            def evacuate(p, i, n, q, m):
                kind, j = TILES[m]
                e = ACT_TILES.index(m)
                act.wait_ge(projected, M * n + m + 1)
                bank = ps[:, m % PROJ_BANKS, 0:TB]
                if kind == "g":
                    if j == 0:
                        need(act, gated, gated_count_before(p, i, 1, "u"))
                    else:
                        need(act, outa_out, 32 * n)
                    act.activation(tmp[:, j, :], bank, ACT.Sigmoid).then_inc(act_evac, 1)
                elif kind == "zb":
                    need(act, zb_out, 32 * n + 16 * j)
                    act.activation(szb[:, :], bank, ACT.Silu).then_inc(act_evac, 1)
                elif kind == "h":
                    if j == 0:
                        act.wait_ge(v_ready, v_count(p, i, 0))
                    else:
                        act.wait_ge(gated, gated_count(p, i, 0, "u"))
                    act.activation(tmp[:, 0, :], bank, ACT.Copy).then_inc(act_evac, 1)
                else:
                    if j == 0:
                        act.wait_ge(v_ready, v_count(p, i, 1))
                    else:
                        act.wait_ge(outa_out, 32 * n + 16)
                    act.activation(tmp[:, 1, :], bank, ACT.Silu).then_inc(act_evac, 1)

            def mixed_a_high(L, s):
                w = ln_width(L)
                act.wait_ge(oa_in[s], 8 * (L - s) + 16)
                if isinstance(L, int) and L == 0:
                    act.wait_ge(projected, M * LAST + 11)
                act.activation(MIX[s][:, 1, 0:JT, 0:w], MIX_F32[s][:, 0, 0:JT, 0:w],
                               ACT.Copy).then_inc(a_hi, 1)

            def squares(L, s):
                w = ln_width(L)
                act.wait_ge(ln, ln_event(L, 1))
                act.activation(tb[:, :, 0:w], cb[s][:, 0:2, 0:w], ACT.Square).then_inc(ln_sq, 1)
                act.wait_ge(ln_mean, L + 1)
                act.activation(ta[:, :, 0:w], cb[s][:, 2:4, 0:w], ACT.Square).then_inc(ln_sq, 1)

            def sum_high(L):
                w = ln_width(L)
                act.wait_ge(ln_sum, 2 * L + 2)
                act.activation(ta_split[:, 1, 0:w], ta[:, 0, 0:w], ACT.Copy).then_inc(ln_sum_hi, 1)

            def var_high(L):
                w = ln_width(L)
                act.wait_ge(ln, ln_event(L, 3))
                act.activation(tb_split[:, 1, 0:w], tb[:, 0, 0:w], ACT.Copy).then_inc(ln_var_hi, 1)

            def silus(L, s):
                w = ln_width(L)
                act.wait_ge(ln, ln_event(L, 16))
                for j in range(JT):
                    act.activation(cb[s][:, j, 0:w], cb[s][:, j, 0:w], ACT.Silu, scale=ln_g[:, j:j + 1],
                                   bias=ln_b[:, j:j + 1]).then_inc(ln_silu, 1)

            def mixed_b_high(L, s):
                w = ln_width(L)
                act.wait_ge(ln, ln_event(L, 17))
                if isinstance(L, int) and L == 0:
                    act.wait_ge(projected, M * LAST + 12)
                act.activation(MIX[s][:, 1, JT:, 0:w], cb[s][:, :, 0:w], ACT.Copy).then_inc(b_hi, 1)

            first_ln = {LN_AT["centre"]: [squares], LN_AT["normalise"] + 2: [silus],
                        M - 3: [mixed_a_high], M - 2: [mixed_b_high]}

            def proj_block(p, i, n, q):
                for m in range(-1, M):
                    w = splits_at(p, i, m)
                    if w:
                        weight_high(*w)
                    if m in ACT_TILES:
                        evacuate(p, i, n, q, m)
                    if last(n):
                        for what in first_ln.get(m, []):
                            what(0, 0)
                        if m in (1, M - 4):
                            sum_high(int(m > 1))
                        if m == LN_AT["square_sums"]:
                            var_high(0)
                        continue
                    nxt = following(p, i)
                    if m in SQUARE_AT and nxt[0] == 0:
                        square(n + 1, 1 - q, SQUARE_AT[m])
                    if m == RSTD_AT and nxt[0] == 0:
                        x_mean_square(n + 1)
                    if m in HIGH_AT[nxt[0]]:
                        high(n + 1, 1 - q, HIGH_AT[nxt[0]][m])

            square(0, 0, 0)
            square(0, 0, 1)
            act.wait_ge(ready0, 5)
            x_mean_square(0)
            weight_high(0, 0)
            act.wait_ge(x_spread0, 1)
            act.activation(spread[:, :], ps[:, STAT_BANK, 0:TB], ACT.Copy).then_inc(x_spread0, 1)
            weight_high(0, 1)
            for r in range(4):
                high_first(r)
            weight_high(0, 2)
            run_blocks(act, proj_block)

            def row_square(R, s, rows):
                act.wait_ge(h_done, R + 1)
                act.activation(out_pair(2)[0:rows, :], hrow[0:rows, s, :], ACT.Square, scale=RMS_SCALE,
                               accum_out=ssq[0:rows, s:s + 1]).then_inc(h_sumsq, 1)

            def step(L, s):
                for r, tile in enumerate(row_tiles(L)):
                    if r == 0 and more(L, 1):
                        squares(L + 1, 1 - s)
                        var_high(L + 1)
                    row_square(*tile)
                    if more(L, 1) and r < 3:
                        (mixed_a_high, silus, mixed_b_high)[r](L + 1, 1 - s)
                    if more(L, 2) and r == 1:
                        sum_high(L + 2)

            run_steps(act, step)

        @block.vector
        def _(dve):
            def low(N, q, h):
                dve.wait_ge(x_hi, 2 * N + h + 3)
                take_low(q, HALF * h, HALF * (h + 1))

            def take_low(q, a, b):
                dve.tensor_tensor(xT[q][:, 1, a:b, :], chunks_of(q, 1, a, b),
                                  xT[q][:, 0, a:b, :].bitcast(F32), ALU.subtract).then_inc(x_lo, 1)

            def weight_low(p, m):
                c = M * p + m
                dve.wait_ge(w_hi, c + 1)
                hi, lo = slot(m)
                dve.tensor_tensor(lo, raw[:, c % 2, :], hi.bitcast(F32), ALU.subtract).then_inc(w_lo_v, 1)

            def window_edges(p, i, n):
                need(dve, taps_done, NT * n)
                if first(i):
                    js = slice(2 * p, 2 * p + 2)
                    need(dve, state_out, 64 * p)
                    dve.tensor_copy(v[:, :, 0:HB], hist_b[:, js, :]).then_inc(edges, 1)
                    dve.memset(v[:, :, HB + SAMPLE:2 * HB + SAMPLE], 0.0).then_inc(edges, 1)
                    dve.tensor_copy(u[:, :, UH0:UH0 + HA], hist_a[:, js, :]).then_inc(edges, 1)
                    dve.memset(u[:, :, UH0 + HA + SAMPLE:P0 + HA], 0.0).then_inc(edges, 1)
                    dve.memset(u[:, :, 0:UH0], 0.0).then_inc(edges, 1)
                else:
                    dve.wait_ge(state_out, 64 * p + 32)
                    dve.tensor_copy(v[:, :, VH:VH + HB], v[:, :, VW - HB:VW]).then_inc(edges, 1)
                    dve.tensor_copy(u[:, :, 0:HA], u[:, :, UW - HA:UW]).then_inc(edges, 1)

            def make_v(p, i, n, q, j):
                if j == 0:
                    dve.wait_ge(edges, edge_count(p, i))
                dve.wait_ge(act_evac, 8 * n + 1 + j)
                dve.wait_ge(projected, M * n + AT["a", j] + 1)
                bank = AT["a", j] % PROJ_BANKS
                parts = [(HB, S0, SAMPLE), (VH + HB + P0, P0, TB - P0)] if first(i) else [(VH + HB, 0, TB)]
                for at, c, w in parts:
                    dve.tensor_tensor(v[:, j, at:at + w], ps[:, bank, c:c + w], tmp[:, j, c:c + w],
                                      ALU.mult).then_inc(v_ready, 1)

            def tap(p, i, n, x):
                j, k = TAPS[x]
                a, w = (0, ACCW) if first(i) else (AC0, TB)
                window, dst = v[:, j, a + k:a + k + w], acc[:, j, a:a + w]
                jj = 2 * p + j
                if k == 0:
                    if j == 0:
                        need(dve, conv_out, 16 * n)
                        if not first(i) or p:
                            dve.wait_ge(conv_out0, 16 * (p + (not first(i))))
                    dve.wait_ge(v_ready, v_count(p, i, j))
                    dve.tensor_scalar(dst, window, wb[:, jj, 0:1], bias_b[:, jj:jj + 1], ALU.mult,
                                      ALU.add).then_inc(taps_done, 1)
                else:
                    dve.wait_ge(taps_done, NT * n + TAP_AT[j, k - 1] + 1)
                    dve.scalar_tensor_tensor(dst, window, wb[:, jj, k:k + 1], dst, ALU.mult,
                                             ALU.add).then_inc(taps_done, 1)

            def conv_a(p, i, n, q, j):
                dve.wait_ge(act_evac, 8 * n + (5 if j == 0 else 7))
                dve.wait_ge(projected, M * n + AT["c", j] + 1)
                bank = AT["c", j] % PROJ_BANKS
                parts = [(UH0 + HA, S0, SAMPLE), (HA + P0, P0, TB - P0)] if first(i) else [(HA, 0, TB)]
                need(dve, gated, gated_count(p, i, j, "u", back=len(parts)))
                for at, c, w in parts:
                    dve.tensor_tensor(u[:, j, at:at + w], ps[:, bank, c:c + w], tmp[:, 0, c:c + w],
                                      ALU.mult).then_inc(gated, 1)
                jj = 2 * p + j
                for k in range(KA):
                    dve.wait_ge(gated, gated_count(p, i, j, "taps", back=KA - k))
                    if k == 0:
                        dve.tensor_scalar(ca[:, :], u[:, j, 0:TB], wa[:, jj, 0:1], None,
                                          ALU.mult).then_inc(gated, 1)
                    else:
                        dve.scalar_tensor_tensor(ca[:, :], u[:, j, k:k + TB], wa[:, jj, k:k + 1],
                                                 ca[:, :], ALU.mult, ALU.add).then_inc(gated, 1)

            def halves(i):
                return [(UH0, S0, SAMPLE), (P0, P0, TB - P0)] if first(i) else [(0, 0, TB)]

            def gate_b(p, i, n, q, j):
                dve.wait_ge(projected, M * n + AT["b", j] + 1)
                dve.wait_ge(gated, gated_count(p, i, j, "taps"))
                bank = AT["b", j] % PROJ_BANKS
                for a, c, w in halves(i):
                    dve.tensor_tensor(ca[:, a:a + w], ps[:, bank, c:c + w], ca[:, a:a + w],
                                      ALU.mult).then_inc(gated, 1)

            def gate_z(p, i, n, q, j):
                dve.wait_ge(act_evac, 8 * n + (6 if j == 0 else 8))
                dve.wait_ge(gated, gated_count(p, i, j, "b"))
                for a, c, w in halves(i):
                    dve.tensor_tensor(tmp[:, 1, c:c + w], ca[:, a:a + w], tmp[:, 1, c:c + w],
                                      ALU.mult).then_inc(gated, 1)

            serve = {AT["a", 0]: (make_v, 0), AT["a", 1]: (make_v, 1), AT["c", 0]: (conv_a, 0),
                     AT["b", 0]: (gate_b, 0), AT["z", 0]: (gate_z, 0), AT["c", 1]: (conv_a, 1),
                     AT["b", 1]: (gate_b, 1), AT["z", 1]: (gate_z, 1)}
            tap_stops_last = {1: 8, 3: 13, 4: 19, 5: 25, 6: 31, 7: 35, 8: 40, 9: 42, 10: 46}

            def chained(L, k, instruction):
                need(dve, ln, ln_event(L, k - 1))
                instruction().then_inc(ln, 1)

            def centre(L, s):
                w = ln_width(L)
                dve.wait_ge(ln_mean, L + 1)
                mean = ps[:, STAT_BANK, 0:w].unsqueeze(1).to_broadcast([P, JT, w])
                chained(L, 1, lambda: dve.tensor_tensor(cb[s][:, :, 0:w], cb[s][:, :, 0:w], mean, ALU.subtract))

            def square_sums(L, s):
                w = ln_width(L)
                dve.wait_ge(ln_sq, 2 * L + 2)
                chained(L, 2, lambda: dve.tensor_tensor(tb[:, :, 0:w], tb[:, :, 0:w], ta[:, :, 0:w], ALU.add))
                chained(L, 3, lambda: dve.tensor_tensor(tb[:, 0, 0:w], tb[:, 0, 0:w], tb[:, 1, 0:w], ALU.add))

            def var_low(L, s):
                w = ln_width(L)
                dve.wait_ge(ln_var_hi, L + 1)
                chained(L, 4, lambda: dve.tensor_tensor(tb_split[:, 0, 0:w], tb[:, 0, 0:w],
                                                        tb_split[:, 1, 0:w].bitcast(F32), ALU.subtract))

            def normalise(L, s):
                w = ln_width(L)
                var, y, t = ps[:, STAT_BANK, 0:w], ta[:, 0, 0:w], ta[:, 1, 0:w]
                dve.wait_ge(ln_var, L + 1)
                chained(L, 5, lambda: dve.tensor_scalar(y, var, LN_EPS, None, ALU.add))
                chained(L, 6, lambda: dve.tensor_scalar(y.bitcast(I32), y.bitcast(I32), -0.5, RSQRT_SEED,
                                                        ALU.mult, ALU.add))
                for k in range(3):
                    chained(L, 7 + 3 * k, lambda: dve.scalar_tensor_tensor(t, y, -0.5, y, ALU.mult, ALU.mult))
                    chained(L, 8 + 3 * k, lambda: dve.scalar_tensor_tensor(t, var, LN_EPS, t, ALU.add, ALU.mult))
                    chained(L, 9 + 3 * k, lambda: dve.scalar_tensor_tensor(y, t, 1.5, y, ALU.add, ALU.mult))
                yb = y.unsqueeze(1).to_broadcast([P, JT, w])
                chained(L, 16, lambda: dve.tensor_tensor(cb[s][:, :, 0:w], cb[s][:, :, 0:w], yb, ALU.mult))

            def gate(L, s):
                w = ln_width(L)
                dve.wait_ge(zt_in[s], 8 * (L - s) + 16)
                dve.wait_ge(ln_silu, 4 * L + 4)
                chained(L, 17, lambda: dve.tensor_tensor(cb[s][:, :, 0:w], cb[s][:, :, 0:w],
                                                         MIX_F32[s][:, 0, JT:, 0:w], ALU.mult))

            def b_low(L, s):
                w = ln_width(L)
                dve.wait_ge(b_hi, L + 1)
                chained(L, 18, lambda: dve.tensor_tensor(MIX[s][:, 0, JT:, 0:w], cb[s][:, :, 0:w],
                                                         MIX[s][:, 1, JT:, 0:w].bitcast(F32), ALU.subtract))

            first_ln = {LN_AT["centre"]: [centre], LN_AT["square_sums"]: [square_sums],
                        LN_AT["var_low"]: [var_low], LN_AT["normalise"]: [normalise], LN_AT["gate"]: [gate],
                        LN_AT["b_low"]: [b_low]}

            taps_left = []

            def take_taps(L, count):
                if isinstance(L, int) and L == 0:
                    for x in taps_left[:count]:
                        tap(PASSES - 1, BLOCKS - 1, LAST, x)
                    del taps_left[:count]

            def proj_block(p, i, n, q):
                done = 0
                stops = tap_stops_last if last(n) else TAP_STOPS
                window_edges(p, i, n)
                for m in range(M):
                    w = splits_at(p, i, m)
                    if w and by_vector(M * w[0] + w[1]):
                        weight_low(*w)
                    if not last(n) and m in LOW_AT[following(p, i)[0]]:
                        low(n + 1, 1 - q, LOW_AT[following(p, i)[0]][m])
                    if last(n):
                        for what in first_ln.get(m, []):
                            what(0, 0)
                    if m in serve:
                        serve[m][0](p, i, n, q, serve[m][1])
                    for x in range(done, stops.get(m, done)):
                        tap(p, i, n, x)
                    done = max(done, stops.get(m, done))
                if not last(n):
                    for x in range(done, NT):
                        tap(p, i, n, x)
                else:
                    taps_left.extend(range(done, NT))

            for h in range(2):
                dve.wait_ge(x_sq, h + 1)
                sq = half_of(0, h, 0)
                dve.tensor_tensor(sq[:, 0:2], sq[:, 0:2], sq[:, 2:4], ALU.add).then_inc(x_sum0, 1)
                dve.wait_ge(x_sum0, 2 * h + 1)
                dve.tensor_tensor(sq[:, 0:1], sq[:, 0:1], sq[:, 1:2], ALU.add).then_inc(x_sum0, 1)
            weight_low(0, 0)
            dve.wait_ge(x_spread0, 2)
            for a, b in QUARTERS[0:2]:
                part = chunks_of(0, 1, a, b)
                dve.tensor_tensor(part, part, spread[:, :].unsqueeze(1).to_broadcast([P, 2, TB]),
                                  ALU.mult).then_inc(x_scaled0, 1)
            for r, (a, b) in enumerate(QUARTERS):
                dve.wait_ge(x_hi, r + 1)
                take_low(0, a, b)
            weight_low(0, 2)
            dve.wait_ge(ready0, 6)
            dve.tensor_copy(mean_w[:, :], mean_w_f32[:, :]).then_inc(mean_w_ready, 1)
            dve.wait_ge(const_in, 112)
            run_blocks(dve, proj_block)

            def add_residual(R, s, rows):
                dve.wait_ge(out_done, R + 1)
                dve.wait_ge(res_in[s], 8 * (R - s) + 16)
                need(dve, y_out[s], 8 * (R - s))
                dve.tensor_tensor(hrow[0:rows, s, :], out_pair(s)[0:rows, :], raw[0:rows, s, :],
                                  ALU.add).then_inc(h_done, 1)

            def finish_rows(R, s, rows):
                dve.wait_ge(h_rstd, R + 1)
                dve.scalar_tensor_tensor(hrow[0:rows, s, :], hrow[0:rows, s, :], rstd[0:rows, s:s + 1],
                                         fgain[0:rows, :], ALU.mult, ALU.mult).then_inc(y_done, 1)

            def step(L, s):
                tiles = row_tiles(L)
                n1, o = not is_last(L), 1 - s
                if n1:
                    centre(L + 1, o)
                take_taps(L, 3)
                if not (isinstance(L, int) and L == 0):
                    finish_rows(RT * L - 1, (RT - 1) % 2, P)
                if n1:
                    square_sums(L + 1, o)
                take_taps(L, 1)
                if n1:
                    var_low(L + 1, o)
                add_residual(*tiles[0])
                if n1:
                    normalise(L + 1, o)
                    finish_rows(*tiles[0])
                take_taps(L, 4)
                if len(tiles) > 1:
                    add_residual(*tiles[1])
                if n1:
                    gate(L + 1, o)
                if len(tiles) > 1:
                    finish_rows(*tiles[1])
                take_taps(L, 4)
                if len(tiles) > 1:
                    add_residual(*tiles[2])
                if n1:
                    b_low(L + 1, o)
                if len(tiles) > 1:
                    finish_rows(*tiles[2])
                take_taps(L, NT)
                if len(tiles) > 1:
                    add_residual(*tiles[3])
                if not n1:
                    finish_rows(*tiles[0])

            dve.wait_ge(fg_in, 16)
            run_steps(dve, step)

        @block.tensor
        def _(pe):
            def split_product(out, terms, start=True, stop=True):
                mm = None
                for x, (ahi, alo, bhi, blo) in enumerate(terms):
                    pe.matmul(out, ahi, bhi, start=(start and x == 0), stop=False)
                    pe.matmul(out, ahi, blo, start=False, stop=False)
                    mm = pe.matmul(out, alo, bhi, start=False, stop=(stop and x == len(terms) - 1))
                return mm

            def x_statistics(N, q):
                if isinstance(N, int) and N == 0:
                    terms = [(0, x_sum0, 2), (HALF, x_sum0, 4)]
                else:
                    terms = [(0, x_sum, 4 * N)]
                sq = xT_f32[q][:, 0].rearrange("p k (r c) -> p k c r", c=STAT_COLS)
                for k, s, count in terms:
                    pe.wait_ge(s, count)
                    for c in range(STAT_COLS):
                        mm = pe.matmul(x_stats(N)[:, c:c + 1], sq[:, k, c, :], ones[:, :],
                                       start=(k == 0), stop=(k == terms[-1][0]))
                mm.then_inc(x_stat, 1)

            def project(p, i, n, q, m):
                if first(i):
                    pe.wait_ge(*weight_split(M * p + m))
                b = (m - PROJ_BANKS) % M
                kind, j = TILES[b]
                if m < PROJ_BANKS:
                    if b in ACT_TILES:
                        need(pe, act_evac, 8 * (n - 1) + ACT_TILES.index(b) + 1)
                    else:
                        need(pe, gated, gated_count_before(p, i, j, "u" if kind == "c" else "b"))
                elif b in ACT_TILES:
                    pe.wait_ge(act_evac, 8 * n + ACT_TILES.index(b) + 1)
                elif kind == "a":
                    pe.wait_ge(v_ready, v_count(p, i, j))
                else:
                    pe.wait_ge(gated, gated_count(p, i, j, "u" if kind == "c" else "b"))
                hi, lo = slot(m)
                x = xT[q]
                begins = isinstance(n, int) and n == 0
                parts = QUARTERS if begins else [(0, HALF), (HALF, KC)]
                for h, (a, b) in enumerate(parts):
                    if m == 0:
                        pe.wait_ge(x_lo, h + 1 if begins else 2 * n + h + 3)
                    mm = split_product(ps[:, m % PROJ_BANKS, 0:TB],
                                       [(hi[:, P * k:P * (k + 1)], lo[:, P * k:P * (k + 1)],
                                         x[:, 0, k, :], x[:, 1, k, :])
                                        for k in range(a, b)], a == 0, b == KC)
                mm.then_inc(projected, 1)

            def channel_mean(L, split, done):
                w, dst = ln_width(L), ps[:, STAT_BANK, :]
                pe.matmul(dst[:, 0:w], mean_w[:, :], split[:, 1, 0:w], start=True, stop=False)
                pe.matmul(dst[:, 0:w], mean_w[:, :], split[:, 0, 0:w], start=False, stop=True).then_inc(done, 1)

            def mean(L):
                pe.wait_ge(ln_sum_lo, L + 1)
                channel_mean(L, ta_split, ln_mean)

            def var(L):
                pe.wait_ge(ln, ln_event(L, 4))
                channel_mean(L, tb_split, ln_var)

            def proj_block(p, i, n, q):
                for m in range(M):
                    if m == RSTD_AT and not last(n) and following(p, i)[0] == 0:
                        x_statistics(n + 1, 1 - q)
                    if last(n) and m == LN_AT["centre"]:
                        pe.wait_ge(mean_w_ready, 1)
                        mean(0)
                    if last(n) and m == LN_AT["normalise"]:
                        var(0)
                    project(p, i, n, q, m)

            pe.wait_ge(ready0, 6)
            x_statistics(0, 0)
            pe.wait_ge(x_rstd, 1)
            to = ps[:, STAT_BANK, 0:TB].rearrange("p (r c) -> p c r", c=STAT_COLS)
            for c in range(STAT_COLS):
                mm = pe.matmul(to[:, c, :], x_rs[0:STAT_ROWS, c:c + 1].to_broadcast([STAT_ROWS, P]),
                               ident[0:STAT_ROWS, 0:STAT_ROWS], start=True, stop=True)
            mm.then_inc(x_spread0, 1)
            run_blocks(pe, proj_block)

            def rows_out(L, s, r, R, rs):
                pe.wait_ge(a_lo, L + 1)
                pe.wait_ge(ln, ln_event(L, LN_OPS))
                need(pe, h_done, R - 1)
                mx = MIX[s]
                for half_d in range(2):
                    cols = slice(512 * half_d, 512 * half_d + 512)
                    terms = []
                    for e in range(KC):
                        hi, lo = slot(e)
                        terms.append((mx[:, 1, e, P * r:P * (r + 1)], mx[:, 0, e, P * r:P * (r + 1)],
                                      hi[:, cols], lo[:, cols]))
                    mm = split_product(ps[:, 2 * rs + half_d, :], terms)
                mm.then_inc(out_done, 1)

            def step(L, s):
                n1 = not is_last(L)
                if n1:
                    mean(L + 1)
                for r, (R, rs, _) in enumerate(row_tiles(L)):
                    rows_out(L, s, r, R, rs)
                    if n1 and r == 0:
                        var(L + 1)

            pe.wait_ge(act_evac, 8 * LAST + ACT_TILES.index(AT["h", 1]) + 1)
            pe.wait_ge(gated, gated_count(1, BLOCKS - 1, 0, "b"))
            pe.wait_ge(*weight_split(M * PASSES + KC - 1))
            run_steps(pe, step)


def kernel(**inputs):
    import numpy as _np
    import concourse.bacc as _bacc
    from concourse import mybir as _mybir
    from concourse.bass_utils import run_bass_kernel_spmd as _run

    c = _np.ascontiguousarray
    g = {k: _np.asarray(a) for k, a in inputs.items()}
    n_tiles = g["w_in"].shape[2] // P
    by_tile = lambda a: c(a.reshape(-1, P).T)
    sample = g["x_sample"][0]
    rows = _np.concatenate([sample[:PAD], sample, g["x_prompt"][0]])
    x_blocks = c(rows.reshape(BLOCKS, TB, 2, HALF, P).transpose(0, 4, 2, 3, 1)).reshape(BLOCKS, P, 2, HALF * TB)
    arrays = {
        "x_prompt": c(g["x_prompt"][0]),
        "xT": x_blocks,
        "x_sample": c(g["x_sample"][0]),
        "state_conv_a": c(g["state_conv_a"][0, 0].T),
        "state_conv_b": c(g["state_conv_b"][0, 0].T),
        "norm_g": by_tile(g["norm_g"][0]),
        "w_in": c(g["w_in"][0].reshape(KC, P, n_tiles, P).transpose(2, 1, 0, 3)).reshape(n_tiles, P, D),
        "conv_a_w": c(g["conv_a_w"][0].T),
        "conv_b_w": c(g["conv_b_w"][0].T),
        "conv_b_bias": by_tile(g["conv_b_bias"][0]),
        "ln_b_g": by_tile(g["ln_b_g"][0]),
        "ln_b_b": by_tile(g["ln_b_b"][0]),
        "w_out": c(g["w_out"][0]),
        "final_norm_g": c(g["final_norm_g"][None, :]),
    }
    outs = {
        "y_prompt": (SEQ, D), "y_sample": (SAMPLE, D),
        "new_a_prompt": (DA, HA), "new_b_prompt": (DA, HB),
        "new_a_sample": (DA, HA), "new_b_sample": (DA, HB),
    }
    nc = _bacc.Bacc("TRN2", target_bir_lowering=False, num_devices=1)
    A, feed = {}, {}
    for name, a in arrays.items():
        feed[f"in_{name}"] = a
        A[name] = nc.dram_tensor(f"in_{name}", a.shape, _mybir.dt.from_np(a.dtype), kind="ExternalInput").ap()
    for name, shape in outs.items():
        A[name] = nc.dram_tensor(f"out_{name}", shape, F32, kind="ExternalOutput").ap()
    build_program(nc, A)
    r = _run(nc, [feed], core_ids=[0]).results[0]
    state = lambda name: c(r[f"out_{name}"].T)[None, None]
    return (r["out_y_prompt"][None], r["out_y_sample"][None], state("new_a_prompt"), state("new_b_prompt"),
            state("new_a_sample"), state("new_b_sample"))
```
